# Optimizing a Trainium2 kernel written in Bass

```python
import math
import jax, jax.numpy as jnp
from jax import lax
import numpy as np

D_MODEL = 1024
BATCH = 1
SEQ = 256
DEPTH = 2

N_A = DEPTH // 2
N_B = DEPTH - N_A

D_FF = ((8 * D_MODEL // 3) + 255) // 256 * 256

RET_DK = 256
RET_HEADS = D_MODEL // RET_DK
RET_DV = 2 * D_MODEL // RET_HEADS
RET_CHUNK = 128
RET_ROT_BASE = 10000.0

ATT_HD = 64
ATT_QH = D_MODEL // ATT_HD
ATT_KVH = ATT_QH // 8
ATT_G = ATT_QH // ATT_KVH
WINDOW = 128
ROPE_THETA = 10000.0

NORM_EPS = 1e-6
NEG_INF = -1e30

kernel_name = "yoco_retention_swa_sink_macaron"

def rms_norm(x, g):
    xf = x.astype(jnp.float32)
    y = xf * lax.rsqrt(jnp.mean(xf * xf, axis=-1, keepdims=True) + NORM_EPS)
    return (y * g.astype(jnp.float32)).astype(x.dtype)

def swiglu(h, w_in, w_out):
    gate, up = jnp.split(h @ w_in, 2, axis=-1)
    return (jax.nn.silu(gate) * up) @ w_out

def rope_half(x):
    s, d = x.shape[1], x.shape[-1]
    inv_freq = 1.0 / (ROPE_THETA ** (jnp.arange(0, d, 2, dtype=jnp.float32) / d))
    ang = jnp.arange(s, dtype=jnp.float32)[:, None] * inv_freq[None, :]
    cos, sin = jnp.cos(ang)[None, :, None, :], jnp.sin(ang)[None, :, None, :]
    xf = x.astype(jnp.float32)
    x1, x2 = xf[..., : d // 2], xf[..., d // 2:]
    return jnp.concatenate([x1 * cos - x2 * sin, x2 * cos + x1 * sin], axis=-1).astype(x.dtype)

def retnet_rotate(x):
    b, s, h, d = x.shape
    freq = 1.0 / (RET_ROT_BASE ** jnp.linspace(0.0, 1.0, d // 2, dtype=jnp.float32))
    ang = jnp.arange(s, dtype=jnp.float32)[:, None] * freq[None, :]
    cos, sin = jnp.cos(ang)[None, :, None, :], jnp.sin(ang)[None, :, None, :]
    xp = x.reshape(b, s, h, d // 2, 2)
    xe, xo = xp[..., 0], xp[..., 1]
    return jnp.stack([xe * cos - xo * sin, xo * cos + xe * sin], axis=-1).reshape(b, s, h, d)

def retention(h, w_in, w_out):
    b, s, _ = h.shape
    nc = s // RET_CHUNK
    dq = RET_HEADS * RET_DK
    dv = RET_HEADS * RET_DV
    q, k, v, g = jnp.split(h @ w_in, [dq, 2 * dq, 2 * dq + dv], axis=-1)
    q = retnet_rotate(q.astype(jnp.float32).reshape(b, s, RET_HEADS, RET_DK))
    k = retnet_rotate(k.astype(jnp.float32).reshape(b, s, RET_HEADS, RET_DK)) * (RET_DK ** -0.5)
    v = v.astype(jnp.float32).reshape(b, s, RET_HEADS, RET_DV)

    log_gamma = jnp.log(1.0 - 2.0 ** (-5.0 - jnp.arange(RET_HEADS, dtype=jnp.float32)))
    n = jnp.arange(RET_CHUNK, dtype=jnp.float32)
    diff = n[:, None] - n[None, :]
    decay_mask = jnp.where(diff[None] >= 0,
                           jnp.exp(jnp.maximum(diff, 0.0)[None] * log_gamma[:, None, None]), 0.0)
    xi = jnp.exp((n[:, None] + 1.0) * log_gamma[None, :])[:, :, None]
    zeta = jnp.exp((RET_CHUNK - 1.0 - n[:, None]) * log_gamma[None, :])[:, :, None]
    chunk_decay = jnp.exp(RET_CHUNK * log_gamma)[:, None, None]

    def to_chunks(t):
        return jnp.moveaxis(t.reshape(b, nc, RET_CHUNK, RET_HEADS, t.shape[-1]), 1, 0)

    def step(state, qkv):
        qc, kc, vc = qkv
        scores = jnp.einsum('bchd,bmhd->bhcm', qc, kc) * decay_mask
        inner = jnp.einsum('bhcm,bmhe->bche', scores, vc)
        cross = jnp.einsum('bchd,bhde->bche', qc, state) * xi
        state = state * chunk_decay + jnp.einsum('bmhd,bmhe->bhde', kc * zeta, vc)
        return state, inner + cross

    state0 = jnp.zeros((b, RET_HEADS, RET_DK, RET_DV), jnp.float32)
    _, out = lax.scan(step, state0, (to_chunks(q), to_chunks(k), to_chunks(v)))
    out = jnp.moveaxis(out, 0, 1).reshape(b, s, RET_HEADS, RET_DV)
    out = out * lax.rsqrt(jnp.mean(out * out, axis=-1, keepdims=True) + NORM_EPS)
    out = out.reshape(b, s, dv).astype(h.dtype) * jax.nn.silu(g)
    return out @ w_out

def shared_kv(x, kv_norm, kv_w, k_norm):
    b, s, _ = x.shape
    k, v = jnp.split(rms_norm(x, kv_norm) @ kv_w, 2, axis=-1)
    k = rope_half(rms_norm(k.reshape(b, s, ATT_KVH, ATT_HD), k_norm))
    v = v.reshape(b, s, ATT_KVH, ATT_HD)
    return k, v

def window_attention(h, k, v, w_q, q_norm, sinks, w_o):
    b, s, _ = h.shape
    nb = s // WINDOW
    q = rope_half(rms_norm((h @ w_q).reshape(b, s, ATT_QH, ATT_HD), q_norm))
    qb = jnp.moveaxis(q.reshape(b, nb, WINDOW, ATT_KVH, ATT_G, ATT_HD), 1, 0)

    def band(t):
        prev = jnp.pad(t, ((0, 0), (WINDOW, 0), (0, 0), (0, 0)))[:, :s]
        cur = t.reshape(b, nb, WINDOW, ATT_KVH, ATT_HD)
        prev = prev.reshape(b, nb, WINDOW, ATT_KVH, ATT_HD)
        return jnp.moveaxis(jnp.concatenate([prev, cur], axis=2), 1, 0)

    kb, vb = band(k), band(v)
    qi = jnp.arange(WINDOW)[:, None]
    kj = jnp.arange(2 * WINDOW)[None, :]
    rel = qi + WINDOW - kj
    sink_logits = jnp.broadcast_to(
        sinks.astype(jnp.float32).reshape(ATT_KVH, ATT_G)[None, :, :, None, None],
        (b, ATT_KVH, ATT_G, WINDOW, 1))
    scale = ATT_HD ** -0.5

    def block(args):
        qx, kx, vx, blk = args
        sc = jnp.einsum('bqkgd,bjkd->bkgqj', qx.astype(jnp.float32), kx.astype(jnp.float32)) * scale
        valid = (rel >= 0) & (rel < WINDOW) & (blk * WINDOW + kj - WINDOW >= 0)
        sc = jnp.where(valid[None, None, None], sc, NEG_INF)
        p = jax.nn.softmax(jnp.concatenate([sc, sink_logits], axis=-1), axis=-1)[..., :-1]
        return jnp.einsum('bkgqj,bjkd->bqkgd', p.astype(vx.dtype), vx)

    o = lax.map(block, (qb, kb, vb, jnp.arange(nb)))
    o = jnp.moveaxis(o, 0, 1).reshape(b, s, ATT_QH * ATT_HD)
    return o @ w_o

def setup_inputs(seed: int = 0) -> dict:
    key = jax.random.key(seed)
    ks = jax.random.split(key, 20)
    f32 = jnp.float32

    def w(k, shape, fan_in):
        return jax.random.normal(k, shape, f32) * (fan_in ** -0.5)

    def gain(k, shape):
        return 1.0 + 0.02 * jax.random.normal(k, shape, f32)

    return {
        "x": jax.random.normal(ks[0], (BATCH, SEQ, D_MODEL), f32),
        "ffn1_norm": gain(ks[1], (DEPTH, D_MODEL)),
        "ffn1_w_in": w(ks[2], (DEPTH, D_MODEL, 2 * D_FF), D_MODEL),
        "ffn1_w_out": w(ks[3], (DEPTH, D_FF, D_MODEL), D_FF),
        "mix_norm": gain(ks[4], (DEPTH, D_MODEL)),
        "ffn2_norm": gain(ks[5], (DEPTH, D_MODEL)),
        "ffn2_w_in": w(ks[6], (DEPTH, D_MODEL, 2 * D_FF), D_MODEL),
        "ffn2_w_out": w(ks[7], (DEPTH, D_FF, D_MODEL), D_FF),
        "ret_w_in": w(ks[8], (N_A, D_MODEL, 2 * RET_HEADS * RET_DK + 2 * RET_HEADS * RET_DV), D_MODEL),
        "ret_w_out": w(ks[9], (N_A, RET_HEADS * RET_DV, D_MODEL), RET_HEADS * RET_DV),
        "kv_norm": gain(ks[10], (D_MODEL,)),
        "kv_w": w(ks[11], (D_MODEL, 2 * ATT_KVH * ATT_HD), D_MODEL),
        "k_norm": gain(ks[12], (ATT_HD,)),
        "attn_w_q": w(ks[13], (N_B, D_MODEL, ATT_QH * ATT_HD), D_MODEL),
        "q_norm": gain(ks[14], (N_B, ATT_HD)),
        "attn_sinks": 0.1 * jax.random.normal(ks[15], (N_B, ATT_QH), f32),
        "attn_w_o": w(ks[16], (N_B, ATT_QH * ATT_HD, D_MODEL), ATT_QH * ATT_HD),
    }

def reference(x, ffn1_norm, ffn1_w_in, ffn1_w_out, mix_norm, ffn2_norm, ffn2_w_in, ffn2_w_out,
              ret_w_in, ret_w_out, kv_norm, kv_w, k_norm, attn_w_q, q_norm, attn_sinks, attn_w_o):
    k_sh, v_sh = None, None
    for i in range(DEPTH):
        x = x + 0.5 * swiglu(rms_norm(x, ffn1_norm[i]), ffn1_w_in[i], ffn1_w_out[i])
        hm = rms_norm(x, mix_norm[i])
        if i < N_A:
            x = x + retention(hm, ret_w_in[i], ret_w_out[i])
        else:
            j = i - N_A
            x = x + window_attention(hm, k_sh, v_sh, attn_w_q[j], q_norm[j], attn_sinks[j], attn_w_o[j])
        x = x + 0.5 * swiglu(rms_norm(x, ffn2_norm[i]), ffn2_w_in[i], ffn2_w_out[i])
        if i == N_A - 1:
            k_sh, v_sh = shared_kv(x, kv_norm, kv_w, k_norm)
    return x


_drawn_inputs = setup_inputs


def setup_inputs(seed=0):
    import zlib

    import numpy as np

    out = dict(_drawn_inputs(seed))
    spreads = {}
    factors = {'ffn1_norm': 3.987,
     'ffn2_norm': 5.566,
     'kv_norm': 8.0,
     'k_norm': 8.0,
     'q_norm': 8.0,
     'attn_sinks': 8.0}
    for name, (base, spread) in spreads.items():
        noise = np.random.default_rng([zlib.crc32(name.encode()), seed]).standard_normal(out[name].shape)
        drawn = base * np.exp(spread * noise) if base else spread * noise
        out[name] = __import__('jax').numpy.asarray(drawn.astype(out[name].dtype))
    for name, factor in factors.items():
        out[name] = (out[name] * factor).astype(out[name].dtype)
    return out
```

```python
import numpy as np

import concourse.bass as bass
from concourse import mybir

F32 = mybir.dt.float32
F32R = mybir.dt.float32r
I32 = mybir.dt.int32
ALU = mybir.AluOpType
ACT = mybir.ActivationFunctionType
AX = mybir.AxisListType
ds = bass.ds

P = 128
T = 256
D = 1024
DT = D // P
F = ((8 * D // 3) + 255) // 256 * 256
FT = F // P
GROUPS = FT // 2
EPS = 1e-6

HEADS_R, DK, DV = 4, 256, 512
YT = HEADS_R * DV // P
HEADS_Q, HD, KVH = 16, 64, 2
CH = 8
NEG = -1e30

SLOTS = 4
UNIT = 2048
OUT_UNIT = FT // 2 * P

PHASES = [("in", 0, 22), ("out", 0, 16), ("ret", 0, 24), ("ret_out", 0, 8), ("in", 1, 22), ("out", 1, 16),
          ("in", 2, 22), ("kv", 0, 1), ("out", 2, 16), ("wq", 0, 4), ("wo", 0, 4), ("in", 3, 22), ("out", 3, 16)]
FIRST, _n = {}, 0
for _kind, _k, _units in PHASES:
    FIRST[_kind, _k] = _n
    _n += _units
UNITS = _n


def columns(u):
    for kind, k, n in PHASES:
        if FIRST[kind, k] <= u < FIRST[kind, k] + n:
            return OUT_UNIT if kind == "out" else UNIT
    return 0


NORMS = 6
KV_GAIN = 6
FFN_NORM = (0, 2, 3, 5)
RET, ATT = 1, 4
CREDIT = 2


class Chain:

    def __init__(self, eng, sem):
        self.eng, self.sem, self.n, self.i, self.per = eng, sem, 0, 0, 0

    def step(self, ins):
        ins.then_inc(self.sem, 1)
        self.n += 1
        self.eng.wait_ge(self.sem, self.n + self.per * self.i)

    def enter(self, i, per):
        self.i, self.per, self.start = i, per, self.n

    def leave(self, times):
        assert self.n - self.start == self.per, (self.n - self.start, self.per)
        self.n = self.start + self.per * times
        self.i = self.per = 0


def trunk(nc, x_t, gains, w_in, w_out, w_ret, w_ret_out, w_kv, w_q, w_o, rot, decay, rope, head_gains,
          mask_c, sinks_c, ident_c, out):
    def at(name, shape, dtype, offset):
        return nc.alloc_sbuf_tensor_at(name, shape, dtype, offset=offset)

    base = 16512
    stage = at("stage", [P, SLOTS, UNIT], F32, base)
    w_hi = at("w_hi", [P, SLOTS, UNIT], F32R, base + 32768)
    w_lo = at("w_lo", [P, SLOTS, UNIT], F32R, base + 65536)
    x = at("x", [P, DT, T], F32, base + 98304)
    h = at("h", [P, DT, 2 * T], F32R, base + 106496)
    big = base + 122880
    act_t = at("act_t", [P, FT, 2 * T], F32R, big)
    y_t = at("y_t", [P, YT, 2 * T], F32R, big)
    q_rot = at("q_rot", [P, 2, T], F32, big + 32768)
    k_rot = at("k_rot", [P, 2, T], F32, big + 34816)
    v_nat = at("v_nat", [P, 2, DV], F32, big + 36864)
    gate = at("gate", [P, 4, T], F32, big + 40960)
    q_nat = at("q_nat", [P, 2, 512], F32, big)
    q_a = at("q_a", [P, 2, 512], F32, big + 4096)
    q_b = at("q_b", [P, 2, 512], F32, big + 8192)
    q_t = at("q_t", [P, 4, T], F32, big + 12288)
    s_own = at("s_own", [P, CH, P], F32, big + 16384)
    s_two = at("s_two", [P, CH, 2 * P], F32, big + 20480)
    pt_own = at("pt_own", [P, CH, 1, P], F32, big + 28672)
    pt_two = at("pt_two", [P, CH, 2, P], F32, big + 32768)
    aux = big + 45056
    ret_cs = at("ret_cs", [P, 2, T], F32, aux)
    q_cs = at("q_cs", [P, 2, T], F32, aux + 2048)
    decay_s = at("decay_s", [P, HEADS_R, T], F32, aux + 4096)
    s_mask = at("s_mask", [P, 384], F32, aux + 8192)
    r_head = at("r_head", [P, T], F32, aux + 9728)
    rot_a = at("rot_a", [P, 2, T], F32, aux + 10752)
    rot_b = at("rot_b", [P, 2, T], F32, aux + 12800)
    h_kv = at("h_kv", [P, DT, 2 * T], F32R, aux)
    kv_nat = at("kv_nat", [P, 2, 2 * KVH * HD], F32, aux)
    k_a = at("k_a", [P, 2, KVH, HD], F32, aux + 2048)
    k_b = at("k_b", [P, 2, KVH, HD], F32, aux + 3072)
    k_pad = at("k_pad", [P, 2, KVH, 2, P], F32, aux + 4096)
    o_t = at("o_t", [P, DT, 2 * T], F32R, aux)
    misc = aux + 16384
    kz = at("kz", [P, KVH, 2, T], F32, misc)
    vz = at("vz", [P, KVH, 2, 2, P], F32, misc + 4096)
    y_f = at("y_f", [P, 4, T], F32, misc)
    y_sq = at("y_sq", [P, 4, T], F32, misc + 4096)
    rope_raw = at("rope_raw", [P, 2, 2, HD], F32, misc)
    gain_raw = at("gain_raw", [P, 2, 2, HD], F32, misc + 1024)
    tmp = at("tmp", [P, 2, 1024], F32, misc + 8192)
    tables = at("tables", [P, 2, 2, 2, HD], F32, misc + 16384)
    mask = at("mask", [P, 2 * P], F32, misc + 18432)
    ident = at("ident", [P, P], F32, misc + 19456)
    ones = at("ones", [P, P], F32, misc + 19968)
    r_row = at("r_row", [P, T], F32, misc + 20480)
    n_v = at("n_v", [P, T], F32, misc + 21504)
    n_t = at("n_t", [P, T], F32, misc + 22528)
    sq_sum = at("sq_sum", [P, T], F32, misc + 23552)
    sq = at("sq", [P, T], F32, misc + 24576)
    gain = at("gain", [P, (NORMS + 1) * DT], F32, misc + 25600)
    sinks = at("sinks", [P, HEADS_Q], F32, misc + 25824)
    r_col = at("r_col", [P, 4], F32, misc + 25888)
    col_v = at("col_v", [P, 4], F32, misc + 25920)
    col_t = at("col_t", [P, 4], F32, misc + 25952)
    hs = [at(f"hs{j}", [P, 16], F32, misc + 25984 + 64 * j) for j in range(3)]
    sm = at("sm", [P, 4, 5, CH], F32, misc + 26176)

    ps = nc.alloc_psum_tensor("ps", [P, 8, 512], F32)
    SUM = 7

    sem = nc.alloc_semaphore
    landed = [sem(f"landed{s}") for s in range(SLOTS)]
    hi_ready, lo_ready = sem("hi_ready"), sem("lo_ready")
    used = sem("used")
    x_loaded, gains_loaded, rot_loaded = sem("x_loaded"), sem("gains_loaded"), sem("rot_loaded")
    rope_loaded, mask_loaded = sem("rope_loaded"), sem("mask_loaded")
    ones_ready, zeroed, tables_ready = sem("ones_ready"), sem("zeroed"), sem("tables_ready")
    sq_done, sum_added = sem("sq_done"), sem("sum_added")
    sum_done, sum_read, r_ready = sem("sum_done"), sem("sum_read"), sem("r_ready")
    h_hi, h_lo = sem("h_hi"), sem("h_lo")
    in_lo_half, in_free = sem("in_lo_half"), sem("in_free")
    in_scaled, in_silu, in_prod, in_hi = sem("in_scaled"), sem("in_silu"), sem("in_prod"), sem("in_hi")
    a_ready = sem("a_ready")
    even_done, out_lo_half, x_done = sem("even_done"), sem("out_lo_half"), sem("x_done")
    pair_lo_half, pair_free = sem("pair_lo_half"), sem("pair_free")
    rot_ready, v_copied = sem("rot_ready"), sem("v_copied")
    score_done, masked, pv_done = sem("score_done"), sem("masked"), sem("pv_done")
    g_scaled, g_silu = sem("g_scaled"), sem("g_silu")
    y_squared, y_half, y_quarter, head_sum = sem("y_squared"), sem("y_half"), sem("y_quarter"), sem("head_sum")
    y_done, y_hi, y_lo = sem("y_done"), sem("y_hi"), sem("y_lo")
    kvh_hi, kvh_lo, kv_copied = sem("kvh_hi"), sem("kvh_lo"), sem("kv_copied")
    vz_ready, kp_ready, kzt_done, kz_ready = sem("vz_ready"), sem("kp_ready"), sem("kzt_done"), sem("kz_ready")
    kp_zeroed = sem("kp_zeroed")
    q_copied, q_roped, qt_done, qt_ready = sem("q_copied"), sem("q_roped"), sem("qt_done"), sem("qt_ready")
    s_done, s_read, max_ready, exp_done, p_ready = (sem("s_done"), sem("s_read"), sem("max_ready"),
                                                    sem("exp_done"), sem("p_ready"))
    pt_done, pt_ready, o_done, o_hi, o_lo = sem("pt_done"), sem("pt_ready"), sem("o_done"), sem("o_hi"), sem("o_lo")
    dve_chain, pool_chain, act_chain = sem("dve_chain"), sem("pool_chain"), sem("act_chain")
    stored = sem("stored")

    def halves(banks):
        return ps[:, banks, 0:T], ps[:, banks, T:2 * T]

    def same(ap, n):
        return ap.rearrange("p (a c) -> p a c", a=1).broadcast_to([P, n, ap.shape[1]])

    with nc.Block() as block:
        @block.sync
        def _(sp):
            def load(src, u, j, i=0):
                if not isinstance(i, int) or u >= SLOTS:
                    sp.wait_ge(lo_ready, u - SLOTS + 1 + 4 * i)
                n = src.shape[2]
                sp.dma_start(stage[:, u % SLOTS, 0:n].rearrange("p (a n) -> p a n", a=1),
                             src[ds(j + 4 * i, 1), :, :].rearrange("a p n -> p a n")).then_inc(landed[u % SLOTS], 16)

            sources = {"in": w_in, "out": w_out, "ret": w_ret, "ret_out": w_ret_out, "kv": w_kv, "wq": w_q, "wo": w_o}
            for kind, k, n in PHASES:
                u, j = FIRST[kind, k], k * n
                peeled = SLOTS if u == 0 else 0
                for e in range(peeled):
                    load(sources[kind], u + e, j + e)
                rounds = (n - peeled) // SLOTS
                if rounds > 1:
                    with sp.Fori(0, rounds) as i:
                        for e in range(SLOTS):
                            load(sources[kind], u + peeled + e, j + peeled + e, i)
                    peeled += rounds * SLOTS
                for e in range(peeled, n):
                    load(sources[kind], u + e, j + e)
            with sp.Fori(0, DT) as d:
                sp.wait_ge(x_done, CREDIT + DT * (NORMS - 1) + 1 + d)
                sp.dma_start(out[:, ds(d, 1), :], x[:, ds(d, 1), :]).then_inc(stored, 16)
            sp.wait_ge(stored, 16 * DT)

        @block.scalar
        def _(act):
            act.dma_start(x[:], x_t).then_inc(x_loaded, 16)
            act.dma_start(gain[:], gains).then_inc(gains_loaded, 16)
            act.dma_start(rope_raw[:], rope).then_inc(rope_loaded, 16)
            act.dma_start(gain_raw[:], head_gains).then_inc(rope_loaded, 16)
            act.dma_start(ret_cs[:], rot).then_inc(rot_loaded, 16)
            act.dma_start(decay_s[:], decay).then_inc(rot_loaded, 16)
            act.dma_start(mask[:], mask_c).then_inc(mask_loaded, 16)
            act.dma_start(sinks[:], sinks_c).then_inc(mask_loaded, 16)
            act.dma_start(ident[:], ident_c).then_inc(mask_loaded, 16)

            def split(u, i=0):
                n, s = columns(u), u % SLOTS
                if not n:
                    return
                if u >= SLOTS:
                    act.wait_ge(used, u - SLOTS + 1 + 4 * i)
                act.wait_ge(landed[s], 16 * (u // SLOTS + 1) + 16 * i)
                nc.scalar.activation(w_hi[:, s, 0:n], stage[:, s, 0:n], ACT.Copy).then_inc(hi_ready, 1)

            def h_hi_tile(m, d, i=0, per=0):
                if m:
                    act.wait_ge(x_done, CREDIT + DT * (m - 1) + d + 1 + per * i)
                act.wait_ge(gains_loaded, 16)
                nc.scalar.activation(h[:, ds(d + per * i, 1), 0:T], x[:, ds(d + per * i, 1), :], ACT.Copy,
                                     scale=gain[:, ds(m * DT + d + per * i, 1)]).then_inc(h_hi, 1)

            def in_evac(f, g, i=0):
                u, c = FIRST["in", f] + 2 * g, GROUPS * f + g + 1 + 2 * i
                act.wait_ge(used, u + 2 + 4 * i)
                act.wait_ge(a_ready, c)
                t = tmp[:, g % 2, :].rearrange("p (o n) -> p o n", o=4)
                nc.scalar.activation(t, ps[:, 4 * (g % 2):4 * (g % 2) + 4, T:2 * T], ACT.Copy).then_inc(in_lo_half, 1)
                split(u + 4, i)
                act.wait_ge(in_scaled, c)
                nc.scalar.activation(tmp[:, g % 2, 0:512], tmp[:, g % 2, 0:512], ACT.Silu).then_inc(in_silu, 1)
                split(u + 5, i)

            def out_evac(n, d, done, units, scale, i=0, per=0):
                c = DT * n + d + 1 + per * i
                if done:
                    act.wait_ge(used, done + 4 * i)
                else:
                    act.wait_ge(even_done, d // 2 + 1)
                act.wait_ge(x_done, c)
                nc.scalar.activation(tmp[:, d % 2, 0:T], ps[:, 4 + d % 2, T:2 * T], ACT.Copy,
                                     scale=scale).then_inc(out_lo_half, 1)
                for u in units[:1]:
                    split(u, i)
                if n + 1 < NORMS:
                    h_hi_tile(n + 1, d, i, per)
                for u in units[1:]:
                    split(u, i)

            def ffn(f):
                m, u = FFN_NORM[f], FIRST["in", f]
                in_evac(f, 0)
                with act.Fori(0, 4) as i:
                    in_evac(f, 1, i)
                    in_evac(f, 2, i)
                if f == 2:
                    for d in range(DT):
                        nc.scalar.activation(h_kv[:, d, 0:T], x[:, d, :], ACT.Copy,
                                             scale=gain[:, KV_GAIN * DT + d:KV_GAIN * DT + d + 1]).then_inc(kvh_hi, 1)
                in_evac(f, 9)
                in_evac(f, 10)
                if f == 2:
                    act.wait_ge(used, FIRST["kv", 0] + 1)
                    act.wait_ge(r_ready, 1)
                    for t in range(2):
                        nc.scalar.activation(kv_nat[:, t, :], ps[:, 6 + t, 0:2 * KVH * HD], ACT.Copy,
                                             scale=r_col[:, 2 * t:2 * t + 1]).then_inc(kv_copied, 1)
                    split(FIRST["kv", 0] + 4)
                u = FIRST["out", f]
                with act.Fori(0, 3) as i:
                    out_evac(m, 0, u + 2, (u + 4, u + 5), 0.5, i, 2)
                    out_evac(m, 1, u + 4, (u + 6, u + 7), 0.5, i, 2)
                out_evac(m, 6, u + 14, (u + 16, u + 17), 0.5)
                out_evac(m, 7, u + 16, (u + 18, u + 19), 0.5)

            def ret_head(hh, i):
                u = FIRST["ret", 0] + 6 * hh
                c = hh + 2 * i

                def s(j):
                    n = columns(u + j)
                    assert n == UNIT
                    sl = (u + j) % SLOTS
                    act.wait_ge(used, u + j - SLOTS + 1 + 12 * i)
                    act.wait_ge(landed[sl], 16 * ((u + j) // SLOTS + 1) + 48 * i)
                    nc.scalar.activation(w_hi[:, sl, :], stage[:, sl, :], ACT.Copy).then_inc(hi_ready, 1)

                def lo_half(j):
                    act.wait_ge(used, u + (1, 2, 5, 6)[j] + 12 * i)
                    b = 2 * (j % 2)
                    if j == 3:
                        b = 0
                    if j == 2:
                        b = 2
                    if j >= 2:
                        act.wait_ge(rot_ready, 2 * c + j - 1)
                    t = tmp[:, j % 2, 0:512].rearrange("p (a n) -> p a n", a=2)
                    nc.scalar.activation(t, ps[:, b:b + 2, T:2 * T], ACT.Copy).then_inc(pair_lo_half, 1)

                def silu(j):
                    act.wait_ge(g_scaled, 2 * c + j - 1)
                    act.wait_ge(y_done, c + 1)
                    t = tmp[:, j % 2, 0:512].rearrange("p (a n) -> p a n", a=2)
                    nc.scalar.activation(gate[:, 2 * (j - 2):2 * (j - 2) + 2, :], t, ACT.Silu).then_inc(g_silu, 1)

                lo_half(0)
                s(4)
                lo_half(1)
                s(5)
                act.wait_ge(used, u + 4 + 12 * i)
                nc.scalar.activation(v_nat[:], ps[:, 0:2, :], ACT.Copy).then_inc(v_copied, 1)
                s(6)
                s(7)
                lo_half(2)
                s(8)
                silu(2)
                act.wait_ge(pv_done, c + 1)
                nc.scalar.activation(y_sq[:].rearrange("p (b a) n -> p b (a n)", b=2), ps[:, 5:7, :],
                                     ACT.Square).then_inc(y_squared, 1)
                lo_half(3)
                s(9)
                silu(3)
                act.wait_ge(y_done, c + 2)
                act.wait_ge(gains_loaded, 16)
                nc.scalar.activation(y_t[:, ds(4 * c, 4), 0:T], y_f[:], ACT.Copy).then_inc(y_hi, 1)

            def attention():
                u = FIRST["wq", 0]
                for c in range(2):
                    act.wait_ge(used, u + 2 * c + 2)
                    if c == 0:
                        act.wait_ge(r_ready, 2)
                    else:
                        act.wait_ge(q_roped, 1)
                    for t in range(2):
                        nc.scalar.activation(q_nat[:, t, :], ps[:, 2 * c + t, :], ACT.Copy,
                                             scale=r_col[:, 2 * t:2 * t + 1]).then_inc(act_chain, 1)
                    act.wait_ge(act_chain, 2 * c + 2)
                    nc.scalar.activation(q_a[:], q_nat[:], ACT.Square).then_inc(q_copied, 1)
                    split(u + 4 + 2 * c)
                    split(u + 5 + 2 * c)
                    if c == 0:
                        act.wait_ge(kzt_done, 1)
                        for t in range(2):
                            nc.scalar.activation(
                                kz[:, :, :, t * P:(t + 1) * P],
                                ps[:, 4 + t, :].rearrange("p (g v n) -> p g v n", g=KVH, v=2),
                                ACT.Copy).then_inc(kz_ready, 1)
                        heads_to_rows(c)
                heads_to_rows(1)

                piece = 0
                for c in range(2):
                    for b in range(2):
                        exps(2 * c + b, c, b)
                        if c or b:
                            piece = rows_of_p(2 * c + b - 1, piece)
                piece = rows_of_p(3, piece)
                u = FIRST["wo", 0]
                for d in range(DT):
                    out_evac(ATT, d, u + d // 2 + 1 if d % 2 else 0, (u + 4 + d // 2,) if d % 2 else (), 1.0)

            def heads_to_rows(c):
                act.wait_ge(qt_done, c + 1)
                if c:
                    act.wait_ge(s_done, 2)
                nc.scalar.activation(q_t[:].rearrange("p (b a) n -> p b (a n)", b=2), ps[:, 4:6, :],
                                     ACT.Copy).then_inc(qt_ready, 1)

            def exps(e, c, b):
                s = s_two if b else s_own
                act.wait_ge(max_ready, e + 1)
                for j in range(CH):
                    nc.scalar.activation(s[:, j, :], s[:, j, :], ACT.Exp, bias=sm[:, e, 1, j:j + 1],
                                         accum_out=sm[:, e, 3, j:j + 1])
                nc.scalar.activation(sm[:, e, 2, :], sm[:, e, 2, :], ACT.Exp).then_inc(exp_done, 1)

            def rows_of_p(e, piece):
                b, c = e % 2, e // 2
                pt = pt_two if b else pt_own
                if c:
                    act.wait_ge(o_done, e - 1)
                for j in range(4 if b else 2):
                    act.wait_ge(pt_done, piece + 1)
                    heads = 4 // (1 + b)
                    nc.scalar.activation(
                        pt[:, heads * j:heads * (j + 1), :, :],
                        ps[:, 4 + piece % 2, :].rearrange("p (a k n) -> p a k n", a=heads, n=P),
                        ACT.Copy).then_inc(pt_ready, 1)
                    piece += 1
                act.wait_ge(o_done, e + 1)
                nc.scalar.activation(o_t[:, 4 * c:4 * c + 4, b * P:(b + 1) * P],
                                     ps[:, 6 + b, :].rearrange("p (a n) -> p a n", a=4), ACT.Copy).then_inc(o_hi, 1)
                return piece

            act.wait_ge(x_loaded, 16)
            split(0)
            with act.Fori(0, 2) as i:
                for d in range(4):
                    h_hi_tile(0, d, i, 4)
            for u in range(1, 4):
                split(u)
            ffn(0)
            with act.Fori(0, 2) as i:
                ret_head(0, i)
                ret_head(1, i)
            u = FIRST["ret_out", 0]
            with act.Fori(0, 2) as i:
                for d in range(4):
                    out_evac(RET, d, u + d + 1, (u + 4 + d,), 1.0, i, 4)
            ffn(1)
            ffn(2)
            attention()
            ffn(3)

        @block.vector
        def _(dve):
            chain = Chain(dve, dve_chain)

            def split(u, i=0, per=4):
                n, s = columns(u), u % SLOTS
                if not n:
                    return
                dve.wait_ge(hi_ready, u + 1 + per * i)
                nc.vector.tensor_tensor(w_lo[:, s, 0:n], stage[:, s, 0:n], w_hi[:, s, 0:n].bitcast(F32),
                                        ALU.subtract).then_inc(lo_ready, 1)

            def rsqrt(v, t, y):
                chain.step(nc.vector.tensor_scalar(t.bitcast(I32), v.bitcast(I32), 1, None, ALU.logical_shift_right))
                chain.step(nc.vector.tensor_scalar(y.bitcast(I32), t.bitcast(I32), -1.0, float(0x5F3759DF),
                                                   ALU.mult, ALU.add))
                for _ in range(3):
                    chain.step(nc.vector.tensor_tensor(t, y, y, ALU.mult))
                    chain.step(nc.vector.scalar_tensor_tensor(t, t, -0.5, v, ALU.mult, ALU.mult))
                    chain.step(nc.vector.scalar_tensor_tensor(y, t, 1.5, y, ALU.add, ALU.mult))

            def token_scale(m):
                dve.wait_ge(sum_done, m + 1)
                ins = nc.vector.tensor_scalar(n_v[:], ps[:, SUM, 0:T], 1.0 / D, EPS, ALU.mult, ALU.add)
                if m in (3, 4):
                    chain.step(ins)
                    ins = nc.vector.tensor_scalar(col_v[:], ps[:, SUM, T:T + 4], 1.0 / D, EPS, ALU.mult, ALU.add)
                ins.then_inc(sum_read, 1)
                dve.wait_ge(sum_read, m + 1)
                if m != ATT:
                    rsqrt(n_v[:], n_t[:], r_row[:])
                if m in (3, 4):
                    rsqrt(col_v[:], col_t[:], r_col[:])
                    nc.vector.tensor_copy(col_t[:], r_col[:]).then_inc(r_ready, 1)

            def h_lo_tile(m, d, i=0, per=0):
                dve.wait_ge(h_hi, DT * m + d + 1 + per * i)
                nc.vector.scalar_tensor_tensor(
                    h[:, ds(d + per * i, 1), T:2 * T], x[:, ds(d + per * i, 1), :],
                    gain[:, ds(m * DT + d + per * i, 1)], h[:, ds(d + per * i, 1), 0:T].bitcast(F32),
                    ALU.mult, ALU.subtract).then_inc(h_lo, 1)

            def in_evac(f, g, i=0):
                u, n = FIRST["in", f] + 2 * g, GROUPS * f + g + 1 + 2 * i
                t = tmp[:, g % 2, :].rearrange("p (o n) -> p o n", o=4)
                dve.wait_ge(in_lo_half, n)
                nc.vector.tensor_tensor(t, ps[:, 4 * (g % 2):4 * (g % 2) + 4, 0:T], t, ALU.add).then_inc(in_free, 1)
                dve.wait_ge(in_free, CREDIT + n)
                nc.vector.tensor_tensor(t, t, same(r_row[:], 4), ALU.mult).then_inc(in_scaled, 1)
                split(u + 4, i)
                dve.wait_ge(in_silu, n)
                nc.vector.tensor_tensor(t[:, 0:2, :], t[:, 0:2, :], t[:, 2:4, :], ALU.mult).then_inc(in_prod, 1)
                dve.wait_ge(in_prod, n)
                hi = act_t[:, ds(2 * g + 4 * i, 2), 0:T]
                nc.vector.tensor_scalar(hi, t[:, 0:2, :], 1.0, None, ALU.mult).then_inc(in_hi, 1)
                dve.wait_ge(in_hi, n)
                nc.vector.tensor_tensor(act_t[:, ds(2 * g + 4 * i, 2), T:2 * T], t[:, 0:2, :], hi.bitcast(F32),
                                        ALU.subtract).then_inc(a_ready, 1)
                split(u + 5, i)

            def out_evac(n, d, units, scale, i=0, per=0):
                c = DT * n + d + 1 + per * i
                dve.wait_ge(out_lo_half, c)
                t = tmp[:, d % 2, 0:T]
                chain.step(nc.vector.scalar_tensor_tensor(t, ps[:, 4 + d % 2, 0:T], scale, t, ALU.mult, ALU.add))
                xd = x[:, ds(d + per * i, 1), :]
                nc.vector.tensor_tensor(xd, xd, t.rearrange("p (a n) -> p a n", a=1), ALU.add).then_inc(x_done, 1)
                for u in units[:1]:
                    split(u, i)
                if n + 1 < NORMS:
                    h_lo_tile(n + 1, d, i, per)
                for u in units[1:]:
                    split(u, i)

            def ffn(f):
                m = FFN_NORM[f]
                token_scale(m)
                in_evac(f, 0)
                with dve.Fori(0, 4) as i:
                    in_evac(f, 1, i)
                    in_evac(f, 2, i)
                if f == 2:
                    for d in range(DT):
                        dve.wait_ge(kvh_hi, d + 1)
                        nc.vector.scalar_tensor_tensor(
                            h_kv[:, d, T:2 * T], x[:, d, :], gain[:, KV_GAIN * DT + d:KV_GAIN * DT + d + 1],
                            h_kv[:, d, 0:T].bitcast(F32), ALU.mult, ALU.subtract).then_inc(kvh_lo, 1)
                in_evac(f, 9)
                in_evac(f, 10)
                if f == 2:
                    split(FIRST["kv", 0] + 4)
                    shared_k()
                u = FIRST["out", f]
                with dve.Fori(0, 3) as i:
                    chain.enter(i, 2)
                    out_evac(m, 0, (u + 4, u + 5), 0.5, i, 2)
                    out_evac(m, 1, (u + 6, u + 7), 0.5, i, 2)
                chain.leave(3)
                out_evac(m, 6, (u + 16, u + 17), 0.5)
                out_evac(m, 7, (u + 18, u + 19), 0.5)

            def head_norm_rope(src, sq_, dst, n, a, b, which, inc):
                ss, sv, sr = (z[:, 0:2 * n] for z in hs)
                chain.step(nc.vector.tensor_reduce(ss, sq_, AX.X, ALU.add))
                chain.step(nc.vector.tensor_scalar(sv, ss, 1.0 / HD, EPS, ALU.mult, ALU.add))
                rsqrt(sv, ss, sr)
                for t in range(2):
                    each = sr[:, n * t:n * (t + 1)].rearrange("p (g a) -> p g a", a=1).broadcast_to([P, n, HD])
                    chain.step(nc.vector.tensor_tensor(src[:, t], src[:, t], each, ALU.mult))
                    cos = same(tables[:, which, 0, t, :], n)
                    sin = tables[:, which, 1, t, :]
                    half = HD // 2
                    chain.step(nc.vector.tensor_tensor(a[:, t], src[:, t], cos, ALU.mult))
                    for k in range(2):
                        o, w = k * half, (1 - k) * half
                        chain.step(nc.vector.tensor_tensor(
                            b[:, t, :, o:o + half], src[:, t, :, w:w + half], same(sin[:, o:o + half], n), ALU.mult))
                for t, d in enumerate(dst):
                    ins = nc.vector.tensor_tensor(d, a[:, t], b[:, t], ALU.add)
                    if t == 0:
                        chain.step(ins)
                inc(ins)

            def shared_k():
                dve.wait_ge(kv_copied, 2)
                dve.wait_ge(tables_ready, 4)
                dve.wait_ge(kp_zeroed, 1)
                k = kv_nat[:, :, 0:KVH * HD].rearrange("p t (h e) -> p t h e", h=KVH)
                chain.step(nc.vector.tensor_tensor(k_a[:], k, k, ALU.mult))
                v0 = k_pad[:, :, :, 0, 0:HD]
                head_norm_rope(k, k_a[:].rearrange("p t h e -> p (t h) e"), [v0[:, t] for t in range(2)], KVH,
                               k_a, k_b, 1, lambda ins: chain.step(ins))
                nc.vector.tensor_copy(k_pad[:, :, :, 1, HD:P], v0).then_inc(kp_ready, 1)

            def ret_head(hh, i):
                u, c = FIRST["ret", 0] + 6 * hh, hh + 2 * i
                t2 = [tmp[:, j, 0:512].rearrange("p (a n) -> p a n", a=2) for j in range(2)]

                def add_halves(j):
                    dve.wait_ge(pair_lo_half, 4 * c + j + 1)
                    b = (0, 2, 2, 0)[j]
                    nc.vector.tensor_tensor(t2[j % 2], ps[:, b:b + 2, 0:T], t2[j % 2], ALU.add).then_inc(pair_free, 1)
                    dve.wait_ge(pair_free, 4 + 4 * c + j + 1)

                def rotate(j, dst, cs):
                    t = t2[j % 2]
                    chain.step(nc.vector.tensor_tensor(rot_a[:], t, same(cs[:, 0, :], 2), ALU.mult))
                    chain.step(nc.vector.tensor_tensor(rot_b[:, 0, :], t[:, 1, :], cs[:, 1, :], ALU.mult))
                    chain.step(nc.vector.tensor_tensor(rot_b[:, 1, :], t[:, 0, :], cs[:, 1, :], ALU.mult))
                    chain.step(nc.vector.tensor_tensor(dst[:, 0, :], rot_a[:, 0, :], rot_b[:, 0, :], ALU.subtract))
                    nc.vector.tensor_tensor(dst[:, 1, :], rot_a[:, 1, :], rot_b[:, 1, :],
                                            ALU.add).then_inc(rot_ready, 1)
                    dve.wait_ge(rot_ready, 2 * c + j + 1)

                def scale_gate(j):
                    nc.vector.tensor_tensor(t2[j % 2], t2[j % 2], same(r_row[:], 2), ALU.mult).then_inc(g_scaled, 1)

                add_halves(0)
                rotate(0, q_rot, q_cs)
                split(u + 4, i, 12)
                add_halves(1)
                rotate(1, k_rot, ret_cs)
                split(u + 5, i, 12)
                split(u + 6, i, 12)
                split(u + 7, i, 12)
                dve.wait_ge(score_done, c + 1)
                dm = decay_s[:, ds(c, 1), :]
                chain.step(nc.vector.tensor_tensor(s_mask[:, 0:T].rearrange("p (a n) -> p a n", a=1),
                                                   ps[:, 4:5, 0:T], dm, ALU.mult))
                nc.vector.tensor_tensor(s_mask[:, T:T + P].rearrange("p (a n) -> p a n", a=1),
                                        ps[:, 4:5, T:T + P], dm[:, :, 0:P], ALU.mult).then_inc(masked, 1)
                add_halves(2)
                scale_gate(2)
                split(u + 8, i, 12)
                add_halves(3)
                scale_gate(3)
                split(u + 9, i, 12)
                dve.wait_ge(head_sum, c + 1)
                chain.step(nc.vector.tensor_scalar(n_v[:], ps[:, SUM, 0:T], 1.0 / DV, EPS, ALU.mult, ALU.add))
                rsqrt(n_v[:], n_t[:], r_head[:])
                chain.step(nc.vector.tensor_tensor(y_f[:].rearrange("p (b a) n -> p b a n", b=2),
                                                   ps[:, 5:7, :].rearrange("p b (a n) -> p b a n", a=2),
                                                   r_head[:].rearrange("p (b a n) -> p b a n", b=1, a=1)
                                                   .broadcast_to([P, 2, 2, T]), ALU.mult))
                dve.wait_ge(g_silu, 2 * c + 2)
                nc.vector.tensor_tensor(y_f[:], y_f[:], gate[:], ALU.mult).then_inc(y_done, 1)
                dve.wait_ge(y_done, c + 2)
                dve.wait_ge(y_hi, c + 1)
                nc.vector.tensor_tensor(y_t[:, ds(4 * c, 4), T:2 * T], y_f[:],
                                        y_t[:, ds(4 * c, 4), 0:T].bitcast(F32), ALU.subtract).then_inc(y_lo, 1)

            def retention():
                token_scale(RET)
                dve.wait_ge(rot_loaded, 32)
                r2 = same(r_row[:], 2)
                chain.step(nc.vector.tensor_tensor(q_cs[:], ret_cs[:], r2, ALU.mult))
                chain.step(nc.vector.scalar_tensor_tensor(ret_cs[:], q_cs[:], float(DK) ** -0.5, r2,
                                                          ALU.mult, ALU.mult))
                with dve.Fori(0, 2) as i:
                    chain.enter(i, 2 * (8 + 1 + 12 + 1))
                    ret_head(0, i)
                    ret_head(1, i)
                chain.leave(2)
                u = FIRST["ret_out", 0]
                with dve.Fori(0, 2) as i:
                    chain.enter(i, 4)
                    for d in range(4):
                        out_evac(RET, d, (u + 4 + d,), 1.0, i, 4)
                chain.leave(2)

            def softmax_front(e):
                c, b = e // 2, e % 2
                s = s_two if b else s_own
                dve.wait_ge(s_done, e + 1)
                if c:
                    dve.wait_ge(pt_done, 2 if b == 0 else 6)
                if b:
                    for j in range(4):
                        ins = nc.vector.scalar_tensor_tensor(
                            s[:, 2 * j:2 * j + 2, :], ps[:, j, :].rearrange("p (a n) -> p a n", a=2), HD ** -0.5,
                            same(mask[:], 2), ALU.mult, ALU.add)
                        if j < 3:
                            chain.step(ins)
                else:
                    for j in range(2):
                        ins = nc.vector.scalar_tensor_tensor(
                            s[:, 4 * j:4 * j + 4, :], ps[:, 6 + j, :].rearrange("p (a n) -> p a n", a=4), HD ** -0.5,
                            same(mask[:, P:2 * P], 4), ALU.mult, ALU.add)
                        if j < 1:
                            chain.step(ins)
                ins.then_inc(s_read, 1)
                dve.wait_ge(s_read, e + 1)
                mx, neg, sk = sm[:, e, 0, :], sm[:, e, 1, :], sm[:, e, 2, :]
                sink = sinks[:, CH * c:CH * c + CH]
                chain.step(nc.vector.tensor_reduce(mx, s[:], AX.X, ALU.max))
                chain.step(nc.vector.tensor_tensor(mx, mx, sink, ALU.max))
                chain.step(nc.vector.tensor_scalar(neg, mx, -1.0, None, ALU.mult))
                nc.vector.tensor_tensor(sk, sink, mx, ALU.subtract).then_inc(max_ready, 1)

            def softmax_back(e):
                s = s_two if e % 2 else s_own
                n = 2 * P if e % 2 else P
                dve.wait_ge(exp_done, e + 1)
                den, rden = sm[:, e, 3, :], sm[:, e, 4, :]
                chain.step(nc.vector.tensor_tensor(den, den, sm[:, e, 2, :], ALU.add))
                chain.step(nc.vector.reciprocal(rden, den))
                nc.vector.tensor_tensor(
                    s[:], s[:], rden.rearrange("p (g a) -> p g a", a=1).broadcast_to([P, CH, n]),
                    ALU.mult).then_inc(p_ready, 1)

            def out_lo(e):
                c, b = e // 2, e % 2
                dve.wait_ge(o_hi, e + 1)
                dst = o_t[:, 4 * c:4 * c + 4, :]
                nc.vector.tensor_tensor(dst[:, :, T + b * P:T + (b + 1) * P],
                                        ps[:, 6 + b, :].rearrange("p (a n) -> p a n", a=4),
                                        dst[:, :, b * P:(b + 1) * P].bitcast(F32), ALU.subtract).then_inc(o_lo, 1)

            def attention():
                token_scale(ATT)
                u = FIRST["wq", 0]
                for c in range(2):
                    dve.wait_ge(q_copied, c + 1)
                    v4 = [z[:].rearrange("p t (h e) -> p t h e", h=CH) for z in (q_nat, q_a, q_b)]
                    if c:
                        dve.wait_ge(qt_done, 1)
                    head_norm_rope(v4[0], v4[1].rearrange("p t h e -> p (t h) e"), [v4[0][:, t] for t in range(2)],
                                   CH, v4[1], v4[2], 0, lambda ins: ins.then_inc(q_roped, 1))
                    split(u + 4 + 2 * c)
                    split(u + 5 + 2 * c)
                dve.wait_ge(mask_loaded, 48)
                softmax_front(0)
                softmax_front(1)
                softmax_back(0)
                softmax_back(1)
                softmax_front(2)
                out_lo(0)
                softmax_front(3)
                softmax_back(2)
                out_lo(1)
                softmax_back(3)
                out_lo(2)
                out_lo(3)
                u = FIRST["wo", 0]
                for d in range(DT):
                    out_evac(ATT, d, (u + 4 + d // 2,) if d % 2 else (), 1.0)

            dve.sem_inc(in_free, CREDIT)
            dve.sem_inc(a_ready, CREDIT)
            dve.sem_inc(x_done, CREDIT)
            dve.sem_inc(pair_free, 4)
            dve.sem_inc(y_done, 1)
            nc.vector.memset(ones[:], 1.0).then_inc(ones_ready, 1)
            dve.wait_ge(x_loaded, 16)
            dve.wait_ge(gains_loaded, 16)
            split(0)
            with dve.Fori(0, 2) as i:
                for d in range(4):
                    h_lo_tile(0, d, i, 4)
            for u in range(1, 4):
                split(u)
            ffn(0)
            retention()
            ffn(1)
            ffn(2)
            attention()
            ffn(3)

        @block.gpsimd
        def _(pool):
            def square_sum(m):
                if m:
                    pool.wait_ge(sum_done, m)
                    pool.wait_ge(x_done, CREDIT + DT * (m - 1) + 1)
                pool.wait_ge(x_loaded, 16)
                nc.gpsimd.tensor_tensor(sq_sum[:], x[:, 0, :], x[:, 0, :], ALU.mult).then_inc(sum_added, 1)
                with pool.Fori(0, DT - 1) as i:
                    pool.wait_ge(sum_added, DT * m + 1 + i)
                    if m:
                        pool.wait_ge(x_done, CREDIT + DT * (m - 1) + 2 + i)
                    pool.wait_ge(x_loaded, 16)
                    nc.gpsimd.tensor_tensor(sq[:].rearrange("p (a n) -> p a n", a=1), x[:, ds(i + 1, 1), :],
                                            x[:, ds(i + 1, 1), :], ALU.mult).then_inc(sq_done, 1)
                    pool.wait_ge(sq_done, (DT - 1) * m + 1 + i)
                    nc.gpsimd.tensor_tensor(sq_sum[:], sq_sum[:], sq[:], ALU.add).then_inc(sum_added, 1)

            square_sum(0)
            pool.wait_ge(rope_loaded, 32)
            for w in range(2):
                for k in range(2):
                    nc.gpsimd.tensor_tensor(tables[:, w, k, :, :], rope_raw[:, k, :, :],
                                            same(gain_raw[:, w, k, :], 2), ALU.mult).then_inc(tables_ready, 1)
            pool.wait_ge(tables_ready, 4)
            square_sum(RET)
            ysf = y_sq[:].rearrange("p a n -> p (a n)")
            with pool.Fori(0, HEADS_R) as i:
                pool.wait_ge(y_squared, i + 1)
                nc.gpsimd.tensor_tensor(ysf[:, 0:512], ysf[:, 0:512], ysf[:, 512:1024], ALU.add).then_inc(y_half, 1)
                pool.wait_ge(y_half, i + 1)
                nc.gpsimd.tensor_tensor(ysf[:, 0:T], ysf[:, 0:T], ysf[:, T:2 * T], ALU.add).then_inc(y_quarter, 1)
            square_sum(2)
            nc.gpsimd.memset(vz[:], 0.0).then_inc(zeroed, 1)
            square_sum(3)
            pool.wait_ge(kv_copied, 2)
            nc.gpsimd.memset(k_pad[:], 0.0).then_inc(kp_zeroed, 1)
            pool.wait_ge(zeroed, 1)
            v = kv_nat[:, :, KVH * HD:2 * KVH * HD].rearrange("p t (g e) -> p t g e", g=KVH)
            for t in range(2):
                for k in range(2):
                    nc.gpsimd.tensor_copy(vz[:, :, t, k, k * HD:(k + 1) * HD], v[:, t]).then_inc(vz_ready, 1)
            square_sum(ATT)
            square_sum(5)

        @block.tensor
        def _(pe):
            def matmul(out_, w, x_, start, stop):
                return nc.tensor.matmul(out_, w, x_, start=start, stop=stop)

            def weight_block(bank, slot, b, moving, first, last):
                cols = slice(b * P, (b + 1) * P)
                matmul(ps[:, bank, :], w_hi[:, slot, cols], moving, first, False)
                return matmul(ps[:, bank, 0:T], w_lo[:, slot, cols], moving[:, 0:T], False, last)

            def token_block(out_, slot, cols, acts, t, first, last):
                hi, lo = acts[:, t * P:(t + 1) * P], acts[:, T + t * P:T + (t + 1) * P]
                matmul(out_, hi, w_hi[:, slot, cols], first, False)
                matmul(out_, lo, w_hi[:, slot, cols], False, False)
                return matmul(out_, hi, w_lo[:, slot, cols], False, last)

            def norm_sum(m):
                pe.wait_ge(sum_added, DT * (m + 1))
                last = matmul(ps[:, SUM, 0:T], ones[:], sq_sum[:], True, True)
                if m in (3, 4):
                    for t in range(2):
                        last = matmul(ps[:, SUM, T + 2 * t:T + 2 * t + 2], sq_sum[:, t * P:(t + 1) * P],
                                      ones[:, 0:2], True, True)
                last.then_inc(sum_done, 1)

            def in_group(f, g, i=0):
                m, u = FFN_NORM[f], FIRST["in", f] + 2 * g
                pe.wait_ge(in_free, GROUPS * f + g + 1 + 2 * i)
                if g == 1:
                    pe.wait_ge(sum_read, m + 1)
                for part in range(2):
                    pe.wait_ge(lo_ready, u + part + 1 + 4 * i)
                    for k in range(4):
                        kt = 4 * part + k
                        if g == 0:
                            pe.wait_ge(h_lo, DT * m + kt + 1)
                        for o in range(4):
                            last = weight_block(4 * (g % 2) + o, (u + part) % SLOTS, 4 * k + o, h[:, kt, :],
                                                kt == 0, kt == DT - 1)
                    if part == 0:
                        last.then_inc(used, 1)
                        if g == 0:
                            norm_sum(m)
                last.then_inc(used, 1)

            def ffn(f):
                m = FFN_NORM[f]
                in_group(f, 0)
                with pe.Fori(0, (GROUPS - 1) // 2) as i:
                    in_group(f, 1, i)
                    in_group(f, 2, i)
                if f == 2:
                    shared_kv()
                pe.wait_ge(in_free, CREDIT + GROUPS * f + GROUPS - 1)
                u0 = FIRST["out", f]
                with pe.Fori(0, DT // 2) as i:
                    for d in range(2):
                        pe.wait_ge(x_done, DT * m + d + 1 + 2 * i)
                        for part in range(2):
                            u = u0 + 2 * d + part
                            pe.wait_ge(lo_ready, u + 1 + 4 * i)
                            for b in range(FT // 2):
                                k = FT // 2 * part + b
                                if d == 0 and k % 2 == 0:
                                    if k in (0, 10, 18, 20):
                                        pe.wait_ge(a_ready, CREDIT + GROUPS * f + {0: 5, 10: 9, 18: 10, 20: 11}[k])
                                last = weight_block(4 + d, u % SLOTS, b, act_t[:, k, :], k == 0, k == FT - 1)
                            last.then_inc(used, 1)

            def shared_kv():
                u = FIRST["kv", 0]
                pe.wait_ge(in_free, CREDIT + GROUPS * 2 + GROUPS - 1)
                pe.wait_ge(kvh_lo, DT)
                pe.wait_ge(lo_ready, u + 1)
                for t in range(2):
                    for k in range(DT):
                        last = token_block(ps[:, 6 + t, 0:2 * KVH * HD], u % SLOTS, slice(256 * k, 256 * (k + 1)),
                                           h_kv[:, k, :], t, k == 0, k == DT - 1)
                last.then_inc(used, 1)

            def pair(u, banks, c, i):
                pe.wait_ge(lo_ready, u + 1 + 12 * i)
                for k in range(DT):
                    for o in range(2):
                        last = weight_block(banks + o, u % SLOTS, 2 * k + o, h[:, k, :], k == 0, k == DT - 1)
                last.then_inc(used, 1)

            def ret_head(hh, i):
                u, c = FIRST["ret", 0] + 6 * hh, hh + 2 * i
                pe.wait_ge(pair_free, 4 * c + 4)
                pair(u, 0, c, i)
                pair(u + 1, 2, c, i)
                pe.wait_ge(pair_free, 4 + 4 * c + 1)
                for part in range(2):
                    pe.wait_ge(lo_ready, u + 3 + part + 12 * i)
                    for t in range(2):
                        for k in range(4):
                            kt = 4 * part + k
                            last = token_block(ps[:, t, :], (u + 2 + part) % SLOTS, slice(512 * k, 512 * (k + 1)),
                                               h[:, kt, :], t, kt == 0, kt == DT - 1)
                    last.then_inc(used, 1)
                pe.wait_ge(rot_ready, 2 * c + 2)
                for kb in range(2):
                    for e in range(2):
                        last = matmul(ps[:, 4, T * kb:T + P * kb], k_rot[:, e, kb * P:(kb + 1) * P],
                                      q_rot[:, e, kb * P:T], e == 0, e == 1)
                last.then_inc(score_done, 1)
                pe.wait_ge(pair_free, 4 + 4 * c + 2)
                pair(u + 4, 2, c, i)
                pe.wait_ge(masked, c + 1)
                pe.wait_ge(v_copied, c + 1)
                pe.wait_ge(y_done, c + 1)
                for e in range(4):
                    o = ps[:, 5 + e // 2, T * (e % 2):T * (e % 2 + 1)]
                    matmul(o, v_nat[:, 0, e * P:(e + 1) * P], s_mask[:, 0:T], True, False)
                    last = matmul(o[:, P:T], v_nat[:, 1, e * P:(e + 1) * P], s_mask[:, T:T + P], False, True)
                last.then_inc(pv_done, 1)
                pair(u + 5, 0, c, i)
                pe.wait_ge(y_quarter, c + 1)
                matmul(ps[:, SUM, 0:T], ones[:], y_sq[:, 0, :], True, True).then_inc(head_sum, 1)

            def retention():
                norm_sum(RET)
                pe.wait_ge(h_lo, DT * (RET + 1))
                pe.wait_ge(sum_read, RET + 1)
                with pe.Fori(0, 2) as i:
                    ret_head(0, i)
                    ret_head(1, i)
                u0 = FIRST["ret_out", 0]
                with pe.Fori(0, 2) as i:
                    for d in range(4):
                        pe.wait_ge(x_done, DT * RET + d + 1 + 4 * i)
                        pe.wait_ge(lo_ready, u0 + d + 1 + 4 * i)
                        for k in range(YT):
                            if d == 0 and k in (0, 12):
                                pe.wait_ge(y_lo, 3 + k // 12)
                            last = weight_block(4 + d % 2, (u0 + d) % SLOTS, k, y_t[:, k, :], k == 0, k == YT - 1)
                        last.then_inc(used, 1)

            def q_unit(c, part):
                u = FIRST["wq", 0] + 2 * c + part
                pe.wait_ge(lo_ready, u + 1)
                for k in range(4):
                    kt = 4 * part + k
                    if c == 0:
                        pe.wait_ge(h_lo, DT * ATT + kt + 1)
                    for t in range(2):
                        last = token_block(ps[:, 2 * c + t, :], u % SLOTS, slice(512 * k, 512 * (k + 1)),
                                           h[:, kt, :], t, kt == 0, kt == DT - 1)
                last.then_inc(used, 1)

            def attention():
                q_unit(0, 0)
                norm_sum(ATT)
                q_unit(0, 1)
                pe.wait_ge(kp_ready, 1)
                pe.wait_ge(mask_loaded, 48)
                for t in range(2):
                    for g in range(KVH):
                        for k in range(2):
                            o = (2 * g + k) * P
                            last = nc.tensor.transpose(ps[:, 4 + t, o:o + P], k_pad[:, t, g, k, :], ident[:])
                last.then_inc(kzt_done, 1)
                q_unit(1, 0)
                q_unit(1, 1)
                pe.wait_ge(vz_ready, 4)
                pe.wait_ge(kz_ready, 2)
                for c in range(2):
                    pe.wait_ge(q_roped, c + 1)
                    if c:
                        pe.wait_ge(qt_ready, 1)
                    for p in range(4):
                        for t in range(2):
                            o = (p % 2) * T + t * P
                            last = nc.tensor.transpose(ps[:, 4 + p // 2, o:o + P], q_nat[:, t, p * P:(p + 1) * P],
                                                       ident[:])
                    last.then_inc(qt_done, 1)
                    pe.wait_ge(qt_ready, c + 1)
                    if c:
                        pe.wait_ge(s_read, 1)
                    else:
                        pe.wait_ge(sum_read, ATT + 1)
                    for p in range(4):
                        last = matmul(ps[:, 6 + p // 2, (p % 2) * T:(p % 2) * T + T], q_t[:, p, 0:P],
                                      kz[:, c, :, 0:P], True, True)
                    last.then_inc(s_done, 1)
                    if c:
                        pe.wait_ge(s_read, 2)
                    else:
                        pe.wait_ge(q_copied, 2)
                    for p in range(4):
                        last = matmul(ps[:, p, :], q_t[:, p, P:T], kz[:, c, :, :], True, True)
                    last.then_inc(s_done, 1)
                piece = 0
                for e in range(4):
                    c, b = e // 2, e % 2
                    s = s_two if b else s_own
                    pt = pt_two if b else pt_own
                    pe.wait_ge(p_ready, e + 1)
                    for j in range(4 * (1 + b) // 2):
                        if piece >= 2:
                            pe.wait_ge(pt_ready, piece - 1)
                        else:
                            pe.wait_ge(qt_ready, 2)
                        for q in range(4):
                            n = 4 * j + q
                            head, kb = (n // 2, n % 2) if b else (n, 0)
                            last = nc.tensor.transpose(ps[:, 4 + piece % 2, q * P:(q + 1) * P],
                                                       s[:, head, kb * P:(kb + 1) * P], ident[:])
                        last.then_inc(pt_done, 1)
                        piece += 1
                    pe.wait_ge(pt_ready, piece)
                    if c:
                        pe.wait_ge(o_lo, e - 1)
                    else:
                        pe.wait_ge(s_read, 3)
                    for p in range(4):
                        n = 0
                        for k in range(2):
                            for kb in range(1 + b):
                                last = matmul(ps[:, 6 + b, p * P:(p + 1) * P], vz[:, c, kb, k, :],
                                              pt[:, 2 * p + k, kb, :], n == 0, n == 2 * (1 + b) - 1)
                                n += 1
                    last.then_inc(o_done, 1)
                u0 = FIRST["wo", 0]
                pe.wait_ge(o_lo, 4)
                for d in range(DT):
                    pe.wait_ge(x_done, DT * ATT + d + 1)
                    u = u0 + d // 2
                    pe.wait_ge(lo_ready, u + 1)
                    for k in range(DT):
                        last = weight_block(4 + d % 2, u % SLOTS, DT * (d % 2) + k, o_t[:, k, :], k == 0, k == DT - 1)
                    last.then_inc(used if d % 2 else even_done, 1)

            pe.wait_ge(ones_ready, 1)
            ffn(0)
            retention()
            ffn(1)
            ffn(2)
            attention()
            ffn(3)


def constants():
    f = np.float32
    freq = (f(1.0) / (f(10000.0) ** np.linspace(0.0, 1.0, DK // 2, dtype=f))).astype(f)
    ang = (np.arange(T, dtype=f)[None, :] * freq[:, None]).astype(f)
    rot = np.stack([np.cos(ang), np.sin(ang)], axis=1).astype(f)
    lg = np.log(1.0 - 2.0 ** (-5.0 - np.arange(HEADS_R, dtype=np.float64)))
    diff = np.arange(T)[None, None, :] - np.arange(P)[:, None, None]
    decay = np.where(diff >= 0, np.exp(np.maximum(diff, 0) * lg[None, :, None]), 0.0).astype(f)
    inv = (f(1.0) / (f(10000.0) ** (np.arange(0, HD, 2, dtype=f) / f(HD)))).astype(f)
    ang = (np.arange(T, dtype=f)[:, None] * inv[None, :]).astype(f)
    cos, sin = np.cos(ang), np.sin(ang)
    rope = np.stack([np.concatenate([cos, cos], 1), np.concatenate([-sin, sin], 1)]).astype(f)
    rope = rope.reshape(2, 2, P, HD).transpose(2, 0, 1, 3)
    rel = np.arange(P)[:, None] + P - np.arange(2 * P)[None, :]
    mask = np.where((rel >= 0) & (rel < P), 0.0, NEG).astype(f)
    return rot, decay, np.ascontiguousarray(rope), mask, np.eye(P, dtype=f)


def kernel(**inputs):
    import concourse.bacc as bacc
    from concourse.bass_utils import run_bass_kernel_spmd

    a = {k: np.asarray(v) for k, v in inputs.items()}
    x_t = a["x"][0].T.reshape(DT, P, T).transpose(1, 0, 2)
    norms = [a["ffn1_norm"][0], a["mix_norm"][0], a["ffn2_norm"][0], a["ffn1_norm"][1], a["mix_norm"][1],
             a["ffn2_norm"][1], a["kv_norm"]]
    gains = np.concatenate([g.reshape(DT, P).T for g in norms], axis=1)
    ins = [a["ffn1_w_in"][0], a["ffn2_w_in"][0], a["ffn1_w_in"][1], a["ffn2_w_in"][1]]
    w_in = np.concatenate([w.reshape(2, 4, P, 2, GROUPS, 2, P).transpose(4, 0, 2, 1, 3, 5, 6).reshape(-1, P, UNIT)
                           for w in ins])
    outs = [a["ffn1_w_out"][0], a["ffn2_w_out"][0], a["ffn1_w_out"][1], a["ffn2_w_out"][1]]
    w_out = np.concatenate([w.reshape(2, FT // 2, P, DT, P).transpose(3, 0, 2, 1, 4).reshape(-1, P, OUT_UNIT)
                            for w in outs])
    wr = a["ret_w_in"][0]
    qk = [wr[:, j * HEADS_R * DK:(j + 1) * HEADS_R * DK].reshape(DT, P, HEADS_R, P, 2).transpose(2, 1, 0, 4, 3)
          .reshape(HEADS_R, 1, P, UNIT) for j in range(2)]
    v, g = (wr[:, 2 * HEADS_R * DK + j * HEADS_R * DV:][:, :HEADS_R * DV] for j in range(2))
    v = v.reshape(2, 4, P, HEADS_R, DV).transpose(3, 0, 2, 1, 4).reshape(HEADS_R, 2, P, UNIT)
    g = g.reshape(DT, P, HEADS_R, 2, 2, P).transpose(2, 3, 1, 0, 4, 5).reshape(HEADS_R, 2, P, UNIT)
    w_ret = np.concatenate([qk[0], qk[1], v, g], axis=1).reshape(-1, P, UNIT)
    w_ret_out = a["ret_w_out"][0].reshape(YT, P, DT, P).transpose(2, 1, 0, 3).reshape(-1, P, UNIT)
    w_kv = a["kv_w"].reshape(DT, P, 2 * KVH * HD).transpose(1, 0, 2).reshape(1, P, UNIT)
    w_q = a["attn_w_q"][0].reshape(2, 4, P, 2, 512).transpose(3, 0, 2, 1, 4).reshape(-1, P, UNIT)
    w_o = a["attn_w_o"][0].reshape(DT, P, DT // 2, 2, P).transpose(2, 1, 3, 0, 4).reshape(-1, P, UNIT)
    rot, decay, rope, mask, ident = constants()
    swapped = [(n, np.concatenate([n[HD // 2:], n[:HD // 2]])) for n in (a["q_norm"][0], a["k_norm"])]
    head_gains = np.broadcast_to(np.stack([np.stack(s) for s in swapped])[None], (P, 2, 2, HD))
    sinks = np.broadcast_to(a["attn_sinks"][0][None], (P, HEADS_Q))

    arrays = dict(x_t=x_t, gains=gains, w_in=w_in, w_out=w_out, w_ret=w_ret, w_ret_out=w_ret_out, w_kv=w_kv,
                  w_q=w_q, w_o=w_o, rot=rot, decay=decay, rope=rope, head_gains=head_gains, mask=mask, sinks=sinks,
                  ident=ident)
    nc = bacc.Bacc("TRN2", target_bir_lowering=False, num_devices=1)
    feeds, args = {}, []
    for name, arr in arrays.items():
        arr = np.ascontiguousarray(arr)
        feeds[f"{name}_dram"] = arr
        args.append(nc.dram_tensor(f"{name}_dram", arr.shape, mybir.dt.from_np(arr.dtype), kind="ExternalInput").ap())
    out = nc.dram_tensor("out_dram", (P, DT, T), F32, kind="ExternalOutput").ap()
    trunk(nc, *args, out)
    r = run_bass_kernel_spmd(nc, [feeds], core_ids=[0])
    got = r.results[0]["out_dram"]
    return np.ascontiguousarray(got.transpose(2, 1, 0).reshape(1, T, D))
```

```python
import numpy as np

import concourse.bass as bass
from concourse import mybir

F32 = mybir.dt.float32
F32R = mybir.dt.float32r
I32 = mybir.dt.int32
ALU = mybir.AluOpType
ACT = mybir.ActivationFunctionType
AX = mybir.AxisListType
ds = bass.ds

P = 128
T = 256
D = 1024
DT = D // P
F = ((8 * D // 3) + 255) // 256 * 256
FT = F // P
GROUPS = FT // 2
EPS = 1e-6

HEADS_R, DK, DV = 4, 256, 512
YT = HEADS_R * DV // P
HEADS_Q, HD, KVH = 16, 64, 2
CH = 8
NEG = -1e30

SLOTS = 4
UNIT = 2048
OUT_UNIT = FT // 2 * P

PHASES = [("in", 0, 22), ("out", 0, 16), ("ret", 0, 24), ("ret_out", 0, 8), ("in", 1, 22), ("out", 1, 16),
          ("in", 2, 22), ("kv", 0, 1), ("out", 2, 16), ("wq", 0, 4), ("wo", 0, 4), ("in", 3, 22), ("out", 3, 16)]
FIRST, _n = {}, 0
for _kind, _k, _units in PHASES:
    FIRST[_kind, _k] = _n
    _n += _units
UNITS = _n


def columns(u):
    for kind, k, n in PHASES:
        if FIRST[kind, k] <= u < FIRST[kind, k] + n:
            return OUT_UNIT if kind == "out" else UNIT
    return 0


NORMS = 6
KV_GAIN = 6
FFN_NORM = (0, 2, 3, 5)
RET, ATT = 1, 4
HEAD_SUMS = HEADS_R
CREDIT = 2


def sums_before(m):
    return m + (HEAD_SUMS if m > RET else 0)


def added_for(m):
    return DT * (m + 1) + (HEAD_SUMS if m > RET else 0)


class Chain:

    def __init__(self, eng, sem):
        self.eng, self.sem, self.n, self.i, self.per = eng, sem, 0, 0, 0

    def step(self, ins):
        ins.then_inc(self.sem, 1)
        self.n += 1
        self.eng.wait_ge(self.sem, self.n + self.per * self.i)

    def enter(self, i, per):
        self.i, self.per, self.start = i, per, self.n

    def leave(self, times):
        assert self.n - self.start == self.per, (self.n - self.start, self.per)
        self.n = self.start + self.per * times
        self.i = self.per = 0


def trunk(nc, x_t, gains, w_in, w_out, w_ret, w_ret_out, w_kv, w_q, w_o, rot, decay, rope, head_gains,
          mask_c, sinks_c, ident_c, out):
    def at(name, shape, dtype, offset):
        return nc.alloc_sbuf_tensor_at(name, shape, dtype, offset=offset)

    base = 16512
    stage = at("stage", [P, SLOTS, UNIT], F32, base)
    w_hi = at("w_hi", [P, SLOTS, UNIT], F32R, base + 32768)
    w_lo = at("w_lo", [P, SLOTS, UNIT], F32R, base + 65536)
    x = at("x", [P, DT, T], F32, base + 98304)
    h = at("h", [P, DT, 2 * T], F32R, base + 106496)
    big = base + 122880
    act_t = at("act_t", [P, FT, 2 * T], F32R, big)
    y_t = at("y_t", [P, YT, 2 * T], F32R, big)
    q_rot = at("q_rot", [P, 2, T], F32, big + 32768)
    k_rot = at("k_rot", [P, 2, T], F32, big + 34816)
    v_nat = at("v_nat", [P, 2, DV], F32, big + 36864)
    gate = at("gate", [P, 4, T], F32, big + 40960)
    q_nat = at("q_nat", [P, 2, 512], F32, big)
    q_a = at("q_a", [P, 2, 512], F32, big + 4096)
    q_b = at("q_b", [P, 2, 512], F32, big + 8192)
    q_sq = at("q_sq", [P, 2, 512], F32, big + 40960)
    q_t = at("q_t", [P, 4, T], F32, big + 12288)
    s_own = at("s_own", [P, CH, P], F32, big + 16384)
    s_two = at("s_two", [P, CH, 2 * P], F32, big + 20480)
    pt_own = at("pt_own", [P, CH, 1, P], F32, big + 28672)
    pt_two = at("pt_two", [P, CH, 2, P], F32, big + 32768)
    aux = big + 45056
    ret_cs = at("ret_cs", [P, 2, T], F32, aux)
    q_cs = at("q_cs", [P, 2, T], F32, aux + 2048)
    decay_s = at("decay_s", [P, HEADS_R, T], F32, aux + 4096)
    s_mask = at("s_mask", [P, 384], F32, aux + 8192)
    r_head = at("r_head", [P, T], F32, aux + 9728)
    rot_a = at("rot_a", [P, 2, T], F32, aux + 10752)
    rot_b = at("rot_b", [P, 2, T], F32, aux + 12800)
    h_kv = at("h_kv", [P, DT, 2 * T], F32R, aux)
    kv_nat = at("kv_nat", [P, 2, 2 * KVH * HD], F32, aux)
    k_a = at("k_a", [P, 2, KVH, HD], F32, aux + 2048)
    k_b = at("k_b", [P, 2, KVH, HD], F32, aux + 3072)
    k_pad = at("k_pad", [P, 2, KVH, 2, P], F32, aux + 4096)
    o_t = at("o_t", [P, DT, 2 * T], F32R, aux)
    misc = aux + 16384
    kz = at("kz", [P, KVH, 2, T], F32, misc)
    vz = at("vz", [P, KVH, 2, 2, P], F32, misc + 4096)
    y_f = at("y_f", [P, 4, T], F32, misc)
    y_sq = at("y_sq", [P, 4, T], F32, misc + 4096)
    rope_raw = at("rope_raw", [P, 2, 2, HD], F32, misc)
    gain_raw = at("gain_raw", [P, 2, 2, HD], F32, misc + 1024)
    tmp = at("tmp", [P, 2, 1024], F32, misc + 8192)
    tables = at("tables", [P, 2, 2, 2, HD], F32, misc + 16384)
    mask = at("mask", [P, 2 * P], F32, misc + 18432)
    ident = at("ident", [P, P], F32, misc + 19456)
    ones = at("ones", [P, P], F32, misc + 19968)
    r_row = at("r_row", [P, T], F32, misc + 20480)
    n_v = at("n_v", [P, T], F32, misc + 21504)
    n_t = at("n_t", [P, T], F32, misc + 22528)
    sq_sum = at("sq_sum", [P, T], F32, misc + 23552)
    sq = at("sq", [P, T], F32, misc + 24576)
    gain = at("gain", [P, (NORMS + 1) * DT], F32, misc + 25600)
    sinks = at("sinks", [P, HEADS_Q], F32, misc + 25824)
    r_col = at("r_col", [P, 4], F32, misc + 25888)
    col_v = at("col_v", [P, 4], F32, misc + 25920)
    col_t = at("col_t", [P, 4], F32, misc + 25952)
    hs = [at(f"hs{j}", [P, 2 * CH], F32, misc + 25984 + 64 * j) for j in range(4)]
    sm = at("sm", [P, 4, 5, CH], F32, misc + 26240)

    ps = nc.alloc_psum_tensor("ps", [P, 8, 512], F32)
    SUM = 7

    sem = nc.alloc_semaphore
    landed = [sem(f"landed{s}") for s in range(SLOTS)]
    hi_ready, lo_ready = sem("hi_ready"), sem("lo_ready")
    used = sem("used")
    x_loaded = [sem(f"x_loaded{j}") for j in range(4)]
    first_landed = [sem(f"first_landed{j}") for j in range(3)]
    first_hi, first_lo = sem("first_hi"), sem("first_lo")
    gains_loaded, rot_loaded = sem("gains_loaded"), sem("rot_loaded")
    rope_loaded, mask_loaded = sem("rope_loaded"), sem("mask_loaded")
    ones_ready, zeroed, tables_ready = sem("ones_ready"), sem("zeroed"), sem("tables_ready")
    sq_done, sum_added = sem("sq_done"), sem("sum_added")
    sum_done, sum_read, r_ready = sem("sum_done"), sem("sum_read"), sem("r_ready")
    h_hi, h_lo = sem("h_hi"), sem("h_lo")
    in_lo_half, in_free = sem("in_lo_half"), sem("in_free")
    in_scaled, in_silu, in_prod, in_hi = sem("in_scaled"), sem("in_silu"), sem("in_prod"), sem("in_hi")
    a_ready = sem("a_ready")
    tile_done, out_lo_half, x_done = sem("tile_done"), sem("out_lo_half"), sem("x_done")
    pair_lo_half, pair_free = sem("pair_lo_half"), sem("pair_free")
    rot_ready, v_copied = sem("rot_ready"), sem("v_copied")
    score_done, masked, pv_done = sem("score_done"), sem("masked"), sem("pv_done")
    g_scaled, g_silu = sem("g_scaled"), sem("g_silu")
    y_squared, y_half = sem("y_squared"), sem("y_half")
    y_done, y_hi, y_lo = sem("y_done"), sem("y_hi"), sem("y_lo")
    kvh_hi, kvh_lo, kv_copied = sem("kvh_hi"), sem("kvh_lo"), sem("kv_copied")
    vz_ready, kp_ready, kzt_done, kz_ready = sem("vz_ready"), sem("kp_ready"), sem("kzt_done"), sem("kz_ready")
    kp_zeroed = sem("kp_zeroed")
    q_squared, rq_ready = sem("q_squared"), sem("rq_ready")
    q_copied, q_roped, qt_done, qt_ready = sem("q_copied"), sem("q_roped"), sem("qt_done"), sem("qt_ready")
    s_done, s_read, max_ready, exp_done, p_ready = (sem("s_done"), sem("s_read"), sem("max_ready"),
                                                    sem("exp_done"), sem("p_ready"))
    pt_done, pt_ready, o_done, o_hi, o_lo = sem("pt_done"), sem("pt_ready"), sem("o_done"), sem("o_hi"), sem("o_lo")
    dve_chain, pool_chain, act_chain = sem("dve_chain"), sem("pool_chain"), sem("act_chain")
    stored = sem("stored")

    def halves(banks):
        return ps[:, banks, 0:T], ps[:, banks, T:2 * T]

    def same(ap, n):
        return ap.rearrange("p (a c) -> p a c", a=1).broadcast_to([P, n, ap.shape[1]])

    with nc.Block() as block:
        @block.sync
        def _(sp):
            def load(src, u, j, i=0):
                if not isinstance(i, int) or u >= SLOTS:
                    sp.wait_ge(lo_ready, u - SLOTS + 1 + 4 * i)
                n = src.shape[2]
                sp.dma_start(stage[:, u % SLOTS, 0:n].rearrange("p (a n) -> p a n", a=1),
                             src[ds(j + 4 * i, 1), :, :].rearrange("a p n -> p a n")).then_inc(landed[u % SLOTS], 16)

            sources = {"in": w_in, "out": w_out, "ret": w_ret, "ret_out": w_ret_out, "kv": w_kv, "wq": w_q, "wo": w_o}
            for kind, k, n in PHASES:
                u, j = FIRST[kind, k], k * n
                peeled = SLOTS if u == 0 else 0
                if peeled:
                    for q in range(4):
                        cols = slice(q * UNIT // 4, (q + 1) * UNIT // 4)
                        sp.dma_start(stage[:, 0, cols], w_in[0, :, cols]).then_inc(
                            first_landed[q] if q < 3 else landed[0], 16)
                for e in range(1, peeled):
                    load(sources[kind], u + e, j + e)
                rounds = (n - peeled) // SLOTS
                if rounds > 1:
                    with sp.Fori(0, rounds) as i:
                        for e in range(SLOTS):
                            load(sources[kind], u + peeled + e, j + peeled + e, i)
                    peeled += rounds * SLOTS
                for e in range(peeled, n):
                    load(sources[kind], u + e, j + e)
            with sp.Fori(0, DT) as d:
                sp.wait_ge(x_done, CREDIT + DT * (NORMS - 1) + 1 + d)
                sp.dma_start(out[:, ds(d, 1), :], x[:, ds(d, 1), :]).then_inc(stored, 16)
            sp.wait_ge(stored, 16 * DT)

        @block.scalar
        def _(act):
            act.dma_start(gain[:], gains).then_inc(gains_loaded, 16)
            for j in range(4):
                act.dma_start(x[:, 2 * j:2 * j + 2, :], x_t[:, 2 * j:2 * j + 2, :]).then_inc(x_loaded[j], 16)
            act.dma_start(rope_raw[:], rope).then_inc(rope_loaded, 16)
            act.dma_start(gain_raw[:], head_gains).then_inc(rope_loaded, 16)
            act.dma_start(ret_cs[:], rot).then_inc(rot_loaded, 16)
            act.dma_start(decay_s[:], decay).then_inc(rot_loaded, 16)
            act.dma_start(mask[:], mask_c).then_inc(mask_loaded, 16)
            act.dma_start(sinks[:], sinks_c).then_inc(mask_loaded, 16)
            act.dma_start(ident[:], ident_c).then_inc(mask_loaded, 16)

            def split(u, i=0):
                n, s = columns(u), u % SLOTS
                if not n:
                    return
                if u >= SLOTS:
                    act.wait_ge(used, u - SLOTS + 1 + 4 * i)
                act.wait_ge(landed[s], 16 * (u // SLOTS + 1) + 16 * i)
                nc.scalar.activation(w_hi[:, s, 0:n], stage[:, s, 0:n], ACT.Copy).then_inc(hi_ready, 1)

            def h_hi_tile(m, d, i=0, per=0):
                if m:
                    act.wait_ge(x_done, CREDIT + DT * (m - 1) + d + 1 + per * i)
                else:
                    act.wait_ge(x_loaded[d // 2], 16)
                act.wait_ge(gains_loaded, 16)
                nc.scalar.activation(h[:, ds(d + per * i, 1), 0:T], x[:, ds(d + per * i, 1), :], ACT.Copy,
                                     scale=gain[:, ds(m * DT + d + per * i, 1)]).then_inc(h_hi, 1)

            def in_evac(f, g, i=0):
                u, c = FIRST["in", f] + 2 * g, GROUPS * f + g + 1 + 2 * i
                act.wait_ge(used, u + 2 + 4 * i)
                act.wait_ge(a_ready, c)
                t = tmp[:, g % 2, :].rearrange("p (o n) -> p o n", o=4)
                nc.scalar.activation(t, ps[:, 4 * (g % 2):4 * (g % 2) + 4, T:2 * T], ACT.Copy).then_inc(in_lo_half, 1)
                split(u + 4, i)
                act.wait_ge(in_scaled, c)
                nc.scalar.activation(tmp[:, g % 2, 0:512], tmp[:, g % 2, 0:512], ACT.Silu).then_inc(in_silu, 1)
                split(u + 5, i)

            def out_evac(n, d, done, units, scale, i=0, per=0, bank=None):
                c = DT * n + d + 1 + per * i
                bank = 4 + d % 2 if bank is None else bank
                if done:
                    act.wait_ge(used, done + 4 * i)
                else:
                    act.wait_ge(tile_done, d - d // 4 + 1)
                act.wait_ge(x_done, c)
                nc.scalar.activation(tmp[:, d % 2, 0:T], ps[:, bank, T:2 * T], ACT.Copy,
                                     scale=scale).then_inc(out_lo_half, 1)
                for u in units[:1]:
                    split(u, i)
                if n + 1 < NORMS:
                    h_hi_tile(n + 1, d, i, per)
                for u in units[1:]:
                    split(u, i)

            def ffn(f):
                m, u = FFN_NORM[f], FIRST["in", f]
                in_evac(f, 0)
                with act.Fori(0, 4) as i:
                    in_evac(f, 1, i)
                    in_evac(f, 2, i)
                if f == 2:
                    for d in range(DT):
                        nc.scalar.activation(h_kv[:, d, 0:T], x[:, d, :], ACT.Copy,
                                             scale=gain[:, KV_GAIN * DT + d:KV_GAIN * DT + d + 1]).then_inc(kvh_hi, 1)
                in_evac(f, 9)
                in_evac(f, 10)
                if f == 2:
                    act.wait_ge(used, FIRST["kv", 0] + 1)
                    act.wait_ge(r_ready, 1)
                    for t in range(2):
                        nc.scalar.activation(kv_nat[:, t, :], ps[:, 6 + t, 0:2 * KVH * HD], ACT.Copy,
                                             scale=r_col[:, 2 * t:2 * t + 1]).then_inc(kv_copied, 1)
                    split(FIRST["kv", 0] + 4)
                u = FIRST["out", f]
                with act.Fori(0, 3) as i:
                    out_evac(m, 0, u + 2, (u + 4, u + 5), 0.5, i, 2)
                    out_evac(m, 1, u + 4, (u + 6, u + 7), 0.5, i, 2)
                out_evac(m, 6, u + 14, (u + 16, u + 17), 0.5)
                out_evac(m, 7, u + 16, (u + 18, u + 19), 0.5)

            def ret_head(c):
                u = FIRST["ret", 0] + 6 * c

                def lo_half(j):
                    act.wait_ge(used, u + (1, 2, 5, 6)[j])
                    b = (0, 2, 2, 0)[j]
                    if j >= 2:
                        act.wait_ge(rot_ready, 2 * c + j - 1)
                    t = tmp[:, j % 2, 0:512].rearrange("p (a n) -> p a n", a=2)
                    nc.scalar.activation(t, ps[:, b:b + 2, T:2 * T], ACT.Copy).then_inc(pair_lo_half, 1)

                def silu(j):
                    act.wait_ge(g_scaled, 2 * c + j - 1)
                    act.wait_ge(y_done, c + 1)
                    t = tmp[:, j % 2, 0:512].rearrange("p (a n) -> p a n", a=2)
                    nc.scalar.activation(gate[:, 2 * (j - 2):2 * (j - 2) + 2, :], t, ACT.Silu).then_inc(g_silu, 1)

                lo_half(0)
                split(u + 4)
                lo_half(1)
                split(u + 5)
                if c:
                    store_y(c - 1)
                split(u + 6)
                act.wait_ge(used, u + 4)
                nc.scalar.activation(v_nat[:], ps[:, 0:2, :], ACT.Copy).then_inc(v_copied, 1)
                split(u + 7)
                lo_half(2)
                split(u + 8)
                silu(2)
                lo_half(3)
                split(u + 9)
                silu(3)
                act.wait_ge(pv_done, c + 1)
                act.wait_ge(sum_added, added_for(RET) + c)
                nc.scalar.activation(y_sq[:].rearrange("p (b a) n -> p b (a n)", b=2), ps[:, 5:7, :],
                                     ACT.Square).then_inc(y_squared, 1)

            def store_y(c):
                act.wait_ge(y_done, c + 2)
                nc.scalar.activation(y_t[:, 4 * c:4 * c + 4, 0:T], y_f[:], ACT.Copy).then_inc(y_hi, 1)

            def attention():
                u = FIRST["wq", 0]
                for c in range(2):
                    act.wait_ge(used, u + 2 * c + 2)
                    if c == 0:
                        act.wait_ge(r_ready, 2)
                    else:
                        act.wait_ge(q_roped, 1)
                        act.wait_ge(rq_ready, 1)
                    for t in range(2):
                        nc.scalar.activation(q_nat[:, t, :], ps[:, 2 * c + t, :], ACT.Copy,
                                             scale=r_col[:, 2 * t:2 * t + 1]).then_inc(q_copied, 1)
                    act.wait_ge(q_copied, 2 * c + 2)
                    nc.scalar.activation(q_sq[:], q_nat[:], ACT.Square).then_inc(q_squared, 1)
                    if c == 0:
                        split(u + 4)
                        act.wait_ge(kzt_done, 1)
                        for t in range(2):
                            nc.scalar.activation(
                                kz[:, :, :, t * P:(t + 1) * P],
                                ps[:, 4 + t, :].rearrange("p (g v n) -> p g v n", g=KVH, v=2),
                                ACT.Copy).then_inc(kz_ready, 1)
                        heads_to_rows(c)
                        split(u + 5)
                    else:
                        split(u + 6)
                        exps(0, 0, 0)
                        split(u + 7)
                        heads_to_rows(c)

                exps(1, 0, 1)
                piece = rows_of_p(0, 0)
                exps(2, 1, 0)
                piece = rows_of_p(1, piece)
                exps(3, 1, 1)
                piece = rows_of_p(2, piece)
                piece = rows_of_p(3, piece)
                u = FIRST["wo", 0]
                for d in range(DT):
                    out_evac(ATT, d, u + (2, 4)[d // 4] if d % 4 == 3 else 0,
                             (u + 4 + d // 2,) if d % 2 else (), 1.0, bank=d)

            def heads_to_rows(c):
                act.wait_ge(qt_done, c + 1)
                if c:
                    act.wait_ge(s_done, 2)
                nc.scalar.activation(q_t[:].rearrange("p (b a) n -> p b (a n)", b=2), ps[:, 4:6, :],
                                     ACT.Copy).then_inc(qt_ready, 1)

            def exps(e, c, b):
                s = s_two if b else s_own
                act.wait_ge(max_ready, e + 1)
                for j in range(CH):
                    nc.scalar.activation(s[:, j, :], s[:, j, :], ACT.Exp, bias=sm[:, e, 1, j:j + 1],
                                         accum_out=sm[:, e, 3, j:j + 1])
                nc.scalar.activation(sm[:, e, 2, :], sm[:, e, 2, :], ACT.Exp).then_inc(exp_done, 1)

            def rows_of_p(e, piece):
                b, c = e % 2, e // 2
                pt = pt_two if b else pt_own
                if c:
                    act.wait_ge(o_done, e - 1)
                for j in range(4 if b else 2):
                    act.wait_ge(pt_done, piece + 1)
                    heads = 4 // (1 + b)
                    nc.scalar.activation(
                        pt[:, heads * j:heads * (j + 1), :, :],
                        ps[:, 4 + piece % 2, :].rearrange("p (a k n) -> p a k n", a=heads, n=P),
                        ACT.Copy).then_inc(pt_ready, 1)
                    piece += 1
                act.wait_ge(o_done, e + 1)
                nc.scalar.activation(o_t[:, 4 * c:4 * c + 4, b * P:(b + 1) * P],
                                     ps[:, 6 + b, :].rearrange("p (a n) -> p a n", a=4), ACT.Copy).then_inc(o_hi, 1)
                return piece

            for d in range(DT):
                if d < 4:
                    act.wait_ge(first_landed[d] if d < 3 else landed[0], 16)
                    cols = slice(d * UNIT // 4, (d + 1) * UNIT // 4)
                    nc.scalar.activation(w_hi[:, 0, cols], stage[:, 0, cols], ACT.Copy).then_inc(
                        first_hi if d < 3 else hi_ready, 1)
                h_hi_tile(0, d)
            for u in range(1, 4):
                split(u)
            ffn(0)
            for c in range(HEADS_R):
                ret_head(c)
            store_y(HEADS_R - 1)
            u = FIRST["ret_out", 0]
            for d in range(DT):
                out_evac(RET, d, u + d + 1, (u + 4 + d,), 1.0, bank=d)
            ffn(1)
            ffn(2)
            attention()
            ffn(3)

        @block.vector
        def _(dve):
            chain = Chain(dve, dve_chain)

            def split(u, i=0, per=4):
                n, s = columns(u), u % SLOTS
                if not n:
                    return
                dve.wait_ge(hi_ready, u + 1 + per * i)
                nc.vector.tensor_tensor(w_lo[:, s, 0:n], stage[:, s, 0:n], w_hi[:, s, 0:n].bitcast(F32),
                                        ALU.subtract).then_inc(lo_ready, 1)

            def rsqrt(v, t, y):
                chain.step(nc.vector.tensor_scalar(t.bitcast(I32), v.bitcast(I32), 1, None, ALU.logical_shift_right))
                chain.step(nc.vector.tensor_scalar(y.bitcast(I32), t.bitcast(I32), -1.0, float(0x5F3759DF),
                                                   ALU.mult, ALU.add))
                for _ in range(3):
                    chain.step(nc.vector.tensor_tensor(t, y, y, ALU.mult))
                    chain.step(nc.vector.scalar_tensor_tensor(t, t, -0.5, v, ALU.mult, ALU.mult))
                    chain.step(nc.vector.scalar_tensor_tensor(y, t, 1.5, y, ALU.add, ALU.mult))

            def token_scale(m):
                dve.wait_ge(sum_done, sums_before(m) + 1)
                ins = nc.vector.tensor_scalar(n_v[:], ps[:, SUM, 0:T], 1.0 / D, EPS, ALU.mult, ALU.add)
                if m in (3, 4):
                    chain.step(ins)
                    ins = nc.vector.tensor_scalar(col_v[:], ps[:, SUM, T:T + 4], 1.0 / D, EPS, ALU.mult, ALU.add)
                ins.then_inc(sum_read, 1)
                dve.wait_ge(sum_read, sums_before(m) + 1)
                if m != ATT:
                    rsqrt(n_v[:], n_t[:], r_row[:])
                if m in (3, 4):
                    rsqrt(col_v[:], col_t[:], r_col[:])
                    nc.vector.tensor_copy(col_t[:], r_col[:]).then_inc(r_ready, 1)

            def h_lo_tile(m, d, i=0, per=0):
                dve.wait_ge(h_hi, DT * m + d + 1 + per * i)
                nc.vector.scalar_tensor_tensor(
                    h[:, ds(d + per * i, 1), T:2 * T], x[:, ds(d + per * i, 1), :],
                    gain[:, ds(m * DT + d + per * i, 1)], h[:, ds(d + per * i, 1), 0:T].bitcast(F32),
                    ALU.mult, ALU.subtract).then_inc(h_lo, 1)

            def in_evac(f, g, i=0):
                u, n = FIRST["in", f] + 2 * g, GROUPS * f + g + 1 + 2 * i
                t = tmp[:, g % 2, :].rearrange("p (o n) -> p o n", o=4)
                dve.wait_ge(in_lo_half, n)
                nc.vector.tensor_tensor(t, ps[:, 4 * (g % 2):4 * (g % 2) + 4, 0:T], t, ALU.add).then_inc(in_free, 1)
                dve.wait_ge(in_free, CREDIT + n)
                nc.vector.tensor_tensor(t, t, same(r_row[:], 4), ALU.mult).then_inc(in_scaled, 1)
                split(u + 4, i)
                dve.wait_ge(in_silu, n)
                nc.vector.tensor_tensor(t[:, 0:2, :], t[:, 0:2, :], t[:, 2:4, :], ALU.mult).then_inc(in_prod, 1)
                dve.wait_ge(in_prod, n)
                hi = act_t[:, ds(2 * g + 4 * i, 2), 0:T]
                nc.vector.tensor_scalar(hi, t[:, 0:2, :], 1.0, None, ALU.mult).then_inc(in_hi, 1)
                dve.wait_ge(in_hi, n)
                nc.vector.tensor_tensor(act_t[:, ds(2 * g + 4 * i, 2), T:2 * T], t[:, 0:2, :], hi.bitcast(F32),
                                        ALU.subtract).then_inc(a_ready, 1)
                split(u + 5, i)

            def out_evac(n, d, units, scale, i=0, per=0, bank=None):
                c = DT * n + d + 1 + per * i
                bank = 4 + d % 2 if bank is None else bank
                dve.wait_ge(out_lo_half, c)
                t = tmp[:, d % 2, 0:T]
                chain.step(nc.vector.scalar_tensor_tensor(t, ps[:, bank, 0:T], scale, t, ALU.mult, ALU.add))
                xd = x[:, ds(d + per * i, 1), :]
                nc.vector.tensor_tensor(xd, xd, t.rearrange("p (a n) -> p a n", a=1), ALU.add).then_inc(x_done, 1)
                for u in units[:1]:
                    split(u, i)
                if n + 1 < NORMS:
                    h_lo_tile(n + 1, d, i, per)
                for u in units[1:]:
                    split(u, i)

            def ffn(f):
                m = FFN_NORM[f]
                token_scale(m)
                in_evac(f, 0)
                with dve.Fori(0, 4) as i:
                    in_evac(f, 1, i)
                    in_evac(f, 2, i)
                if f == 2:
                    for d in range(DT):
                        dve.wait_ge(kvh_hi, d + 1)
                        nc.vector.scalar_tensor_tensor(
                            h_kv[:, d, T:2 * T], x[:, d, :], gain[:, KV_GAIN * DT + d:KV_GAIN * DT + d + 1],
                            h_kv[:, d, 0:T].bitcast(F32), ALU.mult, ALU.subtract).then_inc(kvh_lo, 1)
                in_evac(f, 9)
                in_evac(f, 10)
                if f == 2:
                    split(FIRST["kv", 0] + 4)
                    shared_k()
                u = FIRST["out", f]
                with dve.Fori(0, 3) as i:
                    chain.enter(i, 2)
                    out_evac(m, 0, (u + 4, u + 5), 0.5, i, 2)
                    out_evac(m, 1, (u + 6, u + 7), 0.5, i, 2)
                chain.leave(3)
                out_evac(m, 6, (u + 16, u + 17), 0.5)
                out_evac(m, 7, (u + 18, u + 19), 0.5)

            def rope_(src, a, b, n, which, t):
                cos, sin, half = same(tables[:, which, 0, t, :], n), tables[:, which, 1, t, :], HD // 2
                chain.step(nc.vector.tensor_tensor(a, src, cos, ALU.mult))
                for k in range(2):
                    o, w = k * half, (1 - k) * half
                    chain.step(nc.vector.tensor_tensor(b[:, :, o:o + half], src[:, :, w:w + half],
                                                       same(sin[:, o:o + half], n), ALU.mult))
                return nc.vector.tensor_tensor(a, a, b, ALU.add)

            def per_head(ap, n):
                return ap.rearrange("p (g a) -> p g a", a=1).broadcast_to([P, n, HD])

            def shared_k():
                dve.wait_ge(kv_copied, 2)
                dve.wait_ge(tables_ready, 4)
                dve.wait_ge(kp_zeroed, 1)
                k = kv_nat[:, :, 0:KVH * HD].rearrange("p t (h e) -> p t h e", h=KVH)
                ss, sv, sr = (z[:, 0:2 * KVH] for z in hs[:3])
                chain.step(nc.vector.tensor_tensor(k_a[:], k, k, ALU.mult))
                chain.step(nc.vector.tensor_reduce(ss, k_a[:].rearrange("p t h e -> p (t h) e"), AX.X, ALU.add))
                chain.step(nc.vector.tensor_scalar(sv, ss, 1.0 / HD, EPS, ALU.mult, ALU.add))
                rsqrt(sv, ss, sr)
                for t in range(2):
                    chain.step(nc.vector.tensor_tensor(k[:, t], k[:, t], per_head(sr[:, KVH * t:KVH * (t + 1)], KVH),
                                                       ALU.mult))
                    chain.step(rope_(k[:, t], k_a[:, t], k_b[:, t], KVH, 1, t))
                for v in range(2):
                    ins = nc.vector.tensor_copy(k_pad[:, :, :, v, v * HD:(v + 1) * HD], k_a[:])
                    if v == 0:
                        chain.step(ins)
                ins.then_inc(kp_ready, 1)

            def q_rope(c):
                v4 = [z[:].rearrange("p t (h e) -> p t h e", h=CH) for z in (q_nat, q_a, q_b)]
                if c:
                    dve.wait_ge(qt_done, 1)
                dve.wait_ge(q_copied, 2 * c + 2)
                chain.step(rope_(v4[0][:, 0], v4[1][:, 0], v4[2][:, 0], CH, 0, 0))
                rope_(v4[0][:, 1], v4[1][:, 1], v4[2][:, 1], CH, 0, 1).then_inc(q_roped, 1)

            def q_scale(c):
                ss, sv, sr = hs[0][:], hs[1][:], hs[2 + c][:]
                dve.wait_ge(q_squared, c + 1)
                chain.step(nc.vector.tensor_reduce(ss, q_sq[:].rearrange("p t (h e) -> p (t h) e", h=CH),
                                                   AX.X, ALU.add))
                chain.step(nc.vector.tensor_scalar(sv, ss, 1.0, EPS * HD, ALU.mult, ALU.add))
                rsqrt(sv, ss, sr)
                nc.vector.tensor_copy(sv, sr).then_inc(rq_ready, 1)

            def ret_head(c):
                u = FIRST["ret", 0] + 6 * c
                t2 = [tmp[:, j, 0:512].rearrange("p (a n) -> p a n", a=2) for j in range(2)]

                def add_halves(j):
                    dve.wait_ge(pair_lo_half, 4 * c + j + 1)
                    b = (0, 2, 2, 0)[j]
                    nc.vector.tensor_tensor(t2[j % 2], ps[:, b:b + 2, 0:T], t2[j % 2], ALU.add).then_inc(pair_free, 1)
                    dve.wait_ge(pair_free, 4 + 4 * c + j + 1)

                def rotate(j, dst, cs):
                    t = t2[j % 2]
                    chain.step(nc.vector.tensor_tensor(rot_a[:], t, same(cs[:, 0, :], 2), ALU.mult))
                    chain.step(nc.vector.tensor_tensor(rot_b[:, 0, :], t[:, 1, :], cs[:, 1, :], ALU.mult))
                    chain.step(nc.vector.tensor_tensor(rot_b[:, 1, :], t[:, 0, :], cs[:, 1, :], ALU.mult))
                    chain.step(nc.vector.tensor_tensor(dst[:, 0, :], rot_a[:, 0, :], rot_b[:, 0, :], ALU.subtract))
                    nc.vector.tensor_tensor(dst[:, 1, :], rot_a[:, 1, :], rot_b[:, 1, :],
                                            ALU.add).then_inc(rot_ready, 1)
                    dve.wait_ge(rot_ready, 2 * c + j + 1)

                def scale_gate(j):
                    nc.vector.tensor_tensor(t2[j % 2], t2[j % 2], same(r_row[:], 2), ALU.mult).then_inc(g_scaled, 1)

                add_halves(0)
                rotate(0, q_rot, q_cs)
                split(u + 4)
                if c:
                    norm_y(c - 1)
                add_halves(1)
                rotate(1, k_rot, ret_cs)
                split(u + 5)
                if c:
                    store_y(c - 1)
                split(u + 6)
                split(u + 7)
                add_halves(2)
                scale_gate(2)
                split(u + 8)
                dve.wait_ge(score_done, c + 1)
                chain.step(nc.vector.tensor_tensor(s_mask[:, 0:T], ps[:, 4, 0:T], decay_s[:, c, :], ALU.mult))
                nc.vector.tensor_tensor(s_mask[:, T:T + P], ps[:, 4, T:T + P], decay_s[:, c, 0:P],
                                        ALU.mult).then_inc(masked, 1)
                add_halves(3)
                scale_gate(3)
                split(u + 9)

            def norm_y(c):
                n = sums_before(RET) + 1 + c + 1
                dve.wait_ge(sum_done, n)
                nc.vector.tensor_scalar(n_v[:], ps[:, SUM, 0:T], 1.0 / DV, EPS, ALU.mult, ALU.add).then_inc(sum_read, 1)
                dve.wait_ge(sum_read, n)
                rsqrt(n_v[:], n_t[:], r_head[:])
                chain.step(nc.vector.tensor_tensor(y_f[:].rearrange("p (b a) n -> p b a n", b=2),
                                                   ps[:, 5:7, :].rearrange("p b (a n) -> p b a n", a=2),
                                                   r_head[:].rearrange("p (b a n) -> p b a n", b=1, a=1)
                                                   .broadcast_to([P, 2, 2, T]), ALU.mult))
                dve.wait_ge(g_silu, 2 * c + 2)
                nc.vector.tensor_tensor(y_f[:], y_f[:], gate[:], ALU.mult).then_inc(y_done, 1)
                dve.wait_ge(y_done, c + 2)

            def store_y(c):
                dve.wait_ge(y_hi, c + 1)
                nc.vector.tensor_tensor(y_t[:, 4 * c:4 * c + 4, T:2 * T], y_f[:],
                                        y_t[:, 4 * c:4 * c + 4, 0:T].bitcast(F32), ALU.subtract).then_inc(y_lo, 1)

            def retention():
                token_scale(RET)
                dve.wait_ge(rot_loaded, 32)
                r2 = same(r_row[:], 2)
                chain.step(nc.vector.tensor_tensor(q_cs[:], ret_cs[:], r2, ALU.mult))
                chain.step(nc.vector.scalar_tensor_tensor(ret_cs[:], q_cs[:], float(DK) ** -0.5, r2,
                                                          ALU.mult, ALU.mult))
                for c in range(HEADS_R):
                    ret_head(c)
                norm_y(HEADS_R - 1)
                store_y(HEADS_R - 1)
                u = FIRST["ret_out", 0]
                for d in range(DT):
                    out_evac(RET, d, (u + 4 + d,), 1.0, bank=d)

            def softmax_front(e):
                c, b = e // 2, e % 2
                s = s_two if b else s_own
                dve.wait_ge(s_done, e + 1)
                if c:
                    dve.wait_ge(pt_done, 2 if b == 0 else 6)
                for j in range(CH):
                    if b:
                        scores, m_ = ps[:, j // 2, (j % 2) * T:(j % 2 + 1) * T], mask[:]
                    else:
                        scores, m_ = ps[:, 6 + j // 4, (j % 4) * P:(j % 4 + 1) * P], mask[:, P:2 * P]
                    ins = nc.vector.scalar_tensor_tensor(s[:, j, :], scores, hs[2 + c][:, CH * b + j:CH * b + j + 1],
                                                         m_, ALU.mult, ALU.add)
                    if j < CH - 1:
                        chain.step(ins)
                ins.then_inc(s_read, 1)
                dve.wait_ge(s_read, e + 1)
                mx, neg, sk = sm[:, e, 0, :], sm[:, e, 1, :], sm[:, e, 2, :]
                sink = sinks[:, CH * c:CH * c + CH]
                chain.step(nc.vector.tensor_reduce(mx, s[:], AX.X, ALU.max))
                chain.step(nc.vector.tensor_tensor(mx, mx, sink, ALU.max))
                chain.step(nc.vector.tensor_scalar(neg, mx, -1.0, None, ALU.mult))
                nc.vector.tensor_tensor(sk, sink, mx, ALU.subtract).then_inc(max_ready, 1)

            def softmax_back(e):
                s = s_two if e % 2 else s_own
                n = 2 * P if e % 2 else P
                dve.wait_ge(exp_done, e + 1)
                den, rden = sm[:, e, 3, :], sm[:, e, 4, :]
                chain.step(nc.vector.tensor_tensor(den, den, sm[:, e, 2, :], ALU.add))
                chain.step(nc.vector.reciprocal(rden, den))
                nc.vector.tensor_tensor(
                    s[:], s[:], rden.rearrange("p (g a) -> p g a", a=1).broadcast_to([P, CH, n]),
                    ALU.mult).then_inc(p_ready, 1)

            def out_lo(e):
                c, b = e // 2, e % 2
                dve.wait_ge(o_hi, e + 1)
                dst = o_t[:, 4 * c:4 * c + 4, :]
                nc.vector.tensor_tensor(dst[:, :, T + b * P:T + (b + 1) * P],
                                        ps[:, 6 + b, :].rearrange("p (a n) -> p a n", a=4),
                                        dst[:, :, b * P:(b + 1) * P].bitcast(F32), ALU.subtract).then_inc(o_lo, 1)

            def attention():
                token_scale(ATT)
                u = FIRST["wq", 0]
                dve.wait_ge(mask_loaded, 48)
                q_rope(0)
                q_scale(0)
                split(u + 4)
                split(u + 5)
                softmax_front(0)
                q_rope(1)
                split(u + 6)
                softmax_front(1)
                q_scale(1)
                softmax_back(0)
                split(u + 7)
                softmax_back(1)
                softmax_front(2)
                out_lo(0)
                softmax_front(3)
                softmax_back(2)
                out_lo(1)
                softmax_back(3)
                out_lo(2)
                out_lo(3)
                u = FIRST["wo", 0]
                for d in range(DT):
                    out_evac(ATT, d, (u + 4 + d // 2,) if d % 2 else (), 1.0, bank=d)

            dve.sem_inc(in_free, CREDIT)
            dve.sem_inc(a_ready, CREDIT)
            dve.sem_inc(x_done, CREDIT)
            dve.sem_inc(pair_free, 4)
            dve.sem_inc(y_done, 1)
            nc.vector.memset(ones[:], 1.0).then_inc(ones_ready, 1)
            for d in range(DT):
                if d < 4:
                    if d < 3:
                        dve.wait_ge(first_hi, d + 1)
                    else:
                        dve.wait_ge(hi_ready, 1)
                    cols = slice(d * UNIT // 4, (d + 1) * UNIT // 4)
                    nc.vector.tensor_tensor(w_lo[:, 0, cols], stage[:, 0, cols], w_hi[:, 0, cols].bitcast(F32),
                                            ALU.subtract).then_inc(first_lo if d < 3 else lo_ready, 1)
                h_lo_tile(0, d)
            for u in range(1, 4):
                split(u)
            ffn(0)
            retention()
            ffn(1)
            ffn(2)
            attention()
            ffn(3)

        @block.gpsimd
        def _(pool):
            def square_sum(m):
                if m:
                    pool.wait_ge(sum_done, sums_before(m))
                    pool.wait_ge(x_done, CREDIT + DT * (m - 1) + 1)
                else:
                    for j in range(4):
                        pool.wait_ge(x_loaded[j], 16)
                nc.gpsimd.tensor_tensor(sq_sum[:], x[:, 0, :], x[:, 0, :], ALU.mult).then_inc(sum_added, 1)
                with pool.Fori(0, DT - 1) as i:
                    pool.wait_ge(sum_added, added_for(m) - DT + 1 + i)
                    if m:
                        pool.wait_ge(x_done, CREDIT + DT * (m - 1) + 2 + i)
                    pool.wait_ge(x_loaded[3], 16)
                    nc.gpsimd.tensor_tensor(sq[:].rearrange("p (a n) -> p a n", a=1), x[:, ds(i + 1, 1), :],
                                            x[:, ds(i + 1, 1), :], ALU.mult).then_inc(sq_done, 1)
                    pool.wait_ge(sq_done, (DT - 1) * m + 1 + i)
                    nc.gpsimd.tensor_tensor(sq_sum[:], sq_sum[:], sq[:], ALU.add).then_inc(sum_added, 1)

            square_sum(0)
            pool.wait_ge(rope_loaded, 32)
            for w in range(2):
                for k in range(2):
                    nc.gpsimd.tensor_tensor(tables[:, w, k, :, :], rope_raw[:, k, :, :],
                                            same(gain_raw[:, w, k, :], 2), ALU.mult).then_inc(tables_ready, 1)
            pool.wait_ge(tables_ready, 4)
            square_sum(RET)
            ysf = y_sq[:].rearrange("p a n -> p (a n)")
            with pool.Fori(0, HEADS_R) as i:
                pool.wait_ge(y_squared, i + 1)
                nc.gpsimd.tensor_tensor(ysf[:, 0:512], ysf[:, 0:512], ysf[:, 512:1024], ALU.add).then_inc(y_half, 1)
                pool.wait_ge(y_half, i + 1)
                pool.wait_ge(sum_done, sums_before(RET) + 1 + i)
                nc.gpsimd.tensor_tensor(sq_sum[:], ysf[:, 0:T], ysf[:, T:2 * T], ALU.add).then_inc(sum_added, 1)
            square_sum(2)
            nc.gpsimd.memset(vz[:], 0.0).then_inc(zeroed, 1)
            square_sum(3)
            pool.wait_ge(kv_copied, 2)
            nc.gpsimd.memset(k_pad[:], 0.0).then_inc(kp_zeroed, 1)
            pool.wait_ge(zeroed, 1)
            v = kv_nat[:, :, KVH * HD:2 * KVH * HD].rearrange("p t (g e) -> p t g e", g=KVH)
            for t in range(2):
                for k in range(2):
                    nc.gpsimd.tensor_copy(vz[:, :, t, k, k * HD:(k + 1) * HD], v[:, t]).then_inc(vz_ready, 1)
            square_sum(ATT)
            square_sum(5)

        @block.tensor
        def _(pe):
            def matmul(out_, w, x_, start, stop):
                return nc.tensor.matmul(out_, w, x_, start=start, stop=stop)

            def weight_block(bank, slot, b, moving, first, last):
                cols = slice(b * P, (b + 1) * P)
                matmul(ps[:, bank, :], w_hi[:, slot, cols], moving, first, False)
                return matmul(ps[:, bank, 0:T], w_lo[:, slot, cols], moving[:, 0:T], False, last)

            def token_block(out_, slot, cols, acts, t, first, last):
                hi, lo = acts[:, t * P:(t + 1) * P], acts[:, T + t * P:T + (t + 1) * P]
                matmul(out_, hi, w_hi[:, slot, cols], first, False)
                matmul(out_, lo, w_hi[:, slot, cols], False, False)
                return matmul(out_, hi, w_lo[:, slot, cols], False, last)

            def norm_sum(m):
                pe.wait_ge(sum_added, added_for(m))
                last = matmul(ps[:, SUM, 0:T], ones[:], sq_sum[:], True, True)
                if m in (3, 4):
                    for t in range(2):
                        last = matmul(ps[:, SUM, T + 2 * t:T + 2 * t + 2], sq_sum[:, t * P:(t + 1) * P],
                                      ones[:, 0:2], True, True)
                last.then_inc(sum_done, 1)

            def in_group(f, g, i=0):
                m, u = FFN_NORM[f], FIRST["in", f] + 2 * g
                pe.wait_ge(in_free, GROUPS * f + g + 1 + 2 * i)
                if g == 0 and m - 1 in (RET, ATT):
                    pe.wait_ge(x_done, CREDIT + DT * (m - 1) + 4)
                if g == 1:
                    pe.wait_ge(sum_read, sums_before(m) + 1)
                for part in range(2):
                    if u + part:
                        pe.wait_ge(lo_ready, u + part + 1 + 4 * i)
                    for k in range(4):
                        kt = 4 * part + k
                        if u + part == 0:
                            if k < 3:
                                pe.wait_ge(first_lo, k + 1)
                            else:
                                pe.wait_ge(lo_ready, 1)
                        if g == 0:
                            pe.wait_ge(h_lo, DT * m + kt + 1)
                        for o in range(4):
                            last = weight_block(4 * (g % 2) + o, (u + part) % SLOTS, 4 * k + o, h[:, kt, :],
                                                kt == 0, kt == DT - 1)
                    if part == 0:
                        last.then_inc(used, 1)
                        if g == 0:
                            norm_sum(m)
                last.then_inc(used, 1)

            def ffn(f):
                m = FFN_NORM[f]
                in_group(f, 0)
                with pe.Fori(0, (GROUPS - 1) // 2) as i:
                    in_group(f, 1, i)
                    in_group(f, 2, i)
                if f == 2:
                    shared_kv()
                pe.wait_ge(in_free, CREDIT + GROUPS * f + GROUPS - 1)
                u0 = FIRST["out", f]
                with pe.Fori(0, DT // 2) as i:
                    for d in range(2):
                        pe.wait_ge(x_done, DT * m + d + 1 + 2 * i)
                        for part in range(2):
                            u = u0 + 2 * d + part
                            pe.wait_ge(lo_ready, u + 1 + 4 * i)
                            for b in range(FT // 2):
                                k = FT // 2 * part + b
                                if d == 0 and k % 2 == 0:
                                    if k in (0, 10, 18, 20):
                                        pe.wait_ge(a_ready, CREDIT + GROUPS * f + {0: 5, 10: 9, 18: 10, 20: 11}[k])
                                last = weight_block(4 + d, u % SLOTS, b, act_t[:, k, :], k == 0, k == FT - 1)
                            last.then_inc(used, 1)

            def shared_kv():
                u = FIRST["kv", 0]
                pe.wait_ge(in_free, CREDIT + GROUPS * 2 + GROUPS - 1)
                pe.wait_ge(kvh_lo, DT)
                pe.wait_ge(lo_ready, u + 1)
                for t in range(2):
                    for k in range(DT):
                        last = token_block(ps[:, 6 + t, 0:2 * KVH * HD], u % SLOTS, slice(256 * k, 256 * (k + 1)),
                                           h_kv[:, k, :], t, k == 0, k == DT - 1)
                last.then_inc(used, 1)

            def pair(u, banks, c, i):
                pe.wait_ge(lo_ready, u + 1 + 12 * i)
                for k in range(DT):
                    for o in range(2):
                        last = weight_block(banks + o, u % SLOTS, 2 * k + o, h[:, k, :], k == 0, k == DT - 1)
                last.then_inc(used, 1)

            def ret_head(hh, i):
                u, c = FIRST["ret", 0] + 6 * hh, hh + 2 * i
                pe.wait_ge(pair_free, 4 * c + 4)
                pair(u, 0, c, i)
                head_sum(c)
                pair(u + 1, 2, c, i)
                pe.wait_ge(pair_free, 4 + 4 * c + 1)
                for part in range(2):
                    pe.wait_ge(lo_ready, u + 3 + part + 12 * i)
                    for t in range(2):
                        for k in range(4):
                            kt = 4 * part + k
                            last = token_block(ps[:, t, :], (u + 2 + part) % SLOTS, slice(512 * k, 512 * (k + 1)),
                                               h[:, kt, :], t, kt == 0, kt == DT - 1)
                    last.then_inc(used, 1)
                pe.wait_ge(pair_free, 4 + 4 * c + 2)
                pair(u + 4, 2, c, i)
                pe.wait_ge(rot_ready, 2 * c + 2)
                for kb in range(2):
                    for e in range(2):
                        last = matmul(ps[:, 4, T * kb:T + P * kb], k_rot[:, e, kb * P:(kb + 1) * P],
                                      q_rot[:, e, kb * P:T], e == 0, e == 1)
                last.then_inc(score_done, 1)
                pe.wait_ge(v_copied, c + 1)
                pair(u + 5, 0, c, i)
                pe.wait_ge(masked, c + 1)
                pe.wait_ge(y_done, c + 1)
                for e in range(4):
                    o = ps[:, 5 + e // 2, T * (e % 2):T * (e % 2 + 1)]
                    matmul(o, v_nat[:, 0, e * P:(e + 1) * P], s_mask[:, 0:T], True, False)
                    last = matmul(o[:, P:T], v_nat[:, 1, e * P:(e + 1) * P], s_mask[:, T:T + P], False, True)
                last.then_inc(pv_done, 1)

            def head_sum(c):
                pe.wait_ge(sum_added, added_for(RET) + c)
                pe.wait_ge(sum_read, sums_before(RET) + c)
                matmul(ps[:, SUM, 0:T], ones[:], sq_sum[:], True, True).then_inc(sum_done, 1)

            def retention():
                pe.wait_ge(h_lo, DT * (RET + 1))
                with pe.Fori(0, 2) as i:
                    ret_head(0, i)
                    ret_head(1, i)
                u0 = FIRST["ret_out", 0]
                half = YT - YT // HEADS_R
                pe.wait_ge(pair_free, 4 + 4 * HEADS_R)
                pe.wait_ge(y_lo, HEADS_R - 1)
                for d in range(4):
                    pe.wait_ge(lo_ready, u0 + d + 1)
                    for k in range(half):
                        weight_block(d, (u0 + d) % SLOTS, k, y_t[:, k, :], k == 0, False)
                    if d == 0:
                        head_sum(HEADS_R)
                pe.wait_ge(y_lo, HEADS_R)
                for d in range(DT):
                    if d >= 4:
                        pe.wait_ge(lo_ready, u0 + d + 1)
                    for k in range(half if d < 4 else 0, YT):
                        last = weight_block(d, (u0 + d) % SLOTS, k, y_t[:, k, :], k == 0, k == YT - 1)
                    last.then_inc(used, 1)

            def q_unit(c, part):
                u = FIRST["wq", 0] + 2 * c + part
                pe.wait_ge(lo_ready, u + 1)
                for k in range(4):
                    kt = 4 * part + k
                    if c == 0:
                        pe.wait_ge(h_lo, DT * ATT + kt + 1)
                    for t in range(2):
                        last = token_block(ps[:, 2 * c + t, :], u % SLOTS, slice(512 * k, 512 * (k + 1)),
                                           h[:, kt, :], t, kt == 0, kt == DT - 1)
                last.then_inc(used, 1)

            def q_transposes(c):
                pe.wait_ge(q_roped, c + 1)
                if c:
                    pe.wait_ge(qt_ready, 1)
                else:
                    pe.wait_ge(kz_ready, 2)
                for p in range(4):
                    for t in range(2):
                        o = (p % 2) * T + t * P
                        last = nc.tensor.transpose(ps[:, 4 + p // 2, o:o + P], q_a[:, t, p * P:(p + 1) * P], ident[:])
                last.then_inc(qt_done, 1)

            def scores_own(c):
                pe.wait_ge(qt_ready, c + 1)
                if c:
                    pe.wait_ge(s_read, 1)
                else:
                    pe.wait_ge(sum_read, sums_before(ATT) + 1)
                for p in range(4):
                    last = matmul(ps[:, 6 + p // 2, (p % 2) * T:(p % 2) * T + T], q_t[:, p, 0:P],
                                  kz[:, c, :, 0:P], True, True)
                last.then_inc(s_done, 1)

            def scores_two(c):
                if c:
                    pe.wait_ge(s_read, 2)
                else:
                    pe.wait_ge(q_copied, 4)
                for p in range(4):
                    last = matmul(ps[:, p, :], q_t[:, p, P:T], kz[:, c, :, :], True, True)
                last.then_inc(s_done, 1)

            def values(e, piece):
                c, b = e // 2, e % 2
                s = s_two if b else s_own
                pt = pt_two if b else pt_own
                pe.wait_ge(p_ready, e + 1)
                for j in range(2 * (1 + b)):
                    if piece >= 2:
                        pe.wait_ge(pt_ready, piece - 1)
                    else:
                        pe.wait_ge(qt_ready, 2)
                    for q in range(4):
                        n = 4 * j + q
                        head, kb = (n // 2, n % 2) if b else (n, 0)
                        last = nc.tensor.transpose(ps[:, 4 + piece % 2, q * P:(q + 1) * P],
                                                   s[:, head, kb * P:(kb + 1) * P], ident[:])
                    last.then_inc(pt_done, 1)
                    piece += 1
                pe.wait_ge(pt_ready, piece)
                if c:
                    pe.wait_ge(o_lo, e - 1)
                else:
                    pe.wait_ge(s_read, 3)
                for p in range(4):
                    n = 0
                    for k in range(2):
                        for kb in range(1 + b):
                            last = matmul(ps[:, 6 + b, p * P:(p + 1) * P], vz[:, c, kb, k, :],
                                          pt[:, 2 * p + k, kb, :], n == 0, n == 2 * (1 + b) - 1)
                            n += 1
                last.then_inc(o_done, 1)
                return piece

            def wo_unit(j):
                u = FIRST["wo", 0] + j
                pe.wait_ge(lo_ready, u + 1)
                for d in range(4):
                    for k in range(4):
                        kt = 4 * (j % 2) + k
                        last = weight_block(4 * (j // 2) + d, u % SLOTS, 4 * d + k, o_t[:, kt, :],
                                            kt == 0, kt == DT - 1)
                    if j % 2 and d < 3:
                        last.then_inc(tile_done, 1)
                last.then_inc(used, 1)

            def attention():
                q_unit(0, 0)
                norm_sum(ATT)
                q_unit(0, 1)
                pe.wait_ge(kp_ready, 1)
                pe.wait_ge(mask_loaded, 48)
                for t in range(2):
                    for g in range(KVH):
                        for k in range(2):
                            o = (2 * g + k) * P
                            last = nc.tensor.transpose(ps[:, 4 + t, o:o + P], k_pad[:, t, g, k, :], ident[:])
                last.then_inc(kzt_done, 1)
                q_unit(1, 0)
                q_transposes(0)
                q_unit(1, 1)
                pe.wait_ge(vz_ready, 4)
                scores_own(0)
                scores_two(0)
                q_transposes(1)
                scores_own(1)
                piece = values(0, 0)
                scores_two(1)
                piece = values(1, piece)
                pe.wait_ge(o_lo, 2)
                pe.wait_ge(s_read, 4)
                wo_unit(0)
                piece = values(2, piece)
                values(3, piece)
                pe.wait_ge(o_lo, 4)
                wo_unit(1)
                wo_unit(2)
                wo_unit(3)

            pe.wait_ge(ones_ready, 1)
            ffn(0)
            retention()
            ffn(1)
            ffn(2)
            attention()
            ffn(3)


def constants():
    f = np.float32
    freq = (f(1.0) / (f(10000.0) ** np.linspace(0.0, 1.0, DK // 2, dtype=f))).astype(f)
    ang = (np.arange(T, dtype=f)[None, :] * freq[:, None]).astype(f)
    rot = np.stack([np.cos(ang), np.sin(ang)], axis=1).astype(f)
    lg = np.log(1.0 - 2.0 ** (-5.0 - np.arange(HEADS_R, dtype=np.float64)))
    diff = np.arange(T)[None, None, :] - np.arange(P)[:, None, None]
    decay = np.where(diff >= 0, np.exp(np.maximum(diff, 0) * lg[None, :, None]), 0.0).astype(f)
    inv = (f(1.0) / (f(10000.0) ** (np.arange(0, HD, 2, dtype=f) / f(HD)))).astype(f)
    ang = (np.arange(T, dtype=f)[:, None] * inv[None, :]).astype(f)
    cos, sin = np.cos(ang), np.sin(ang)
    rope = np.stack([np.concatenate([cos, cos], 1), np.concatenate([-sin, sin], 1)]).astype(f)
    rope = rope.reshape(2, 2, P, HD).transpose(2, 0, 1, 3)
    rel = np.arange(P)[:, None] + P - np.arange(2 * P)[None, :]
    mask = np.where((rel >= 0) & (rel < P), 0.0, NEG).astype(f)
    return rot, decay, np.ascontiguousarray(rope), mask, np.eye(P, dtype=f)


def kernel(**inputs):
    import concourse.bacc as bacc
    from concourse.bass_utils import run_bass_kernel_spmd

    a = {k: np.asarray(v) for k, v in inputs.items()}
    x_t = a["x"][0].T.reshape(DT, P, T).transpose(1, 0, 2)
    norms = [a["ffn1_norm"][0], a["mix_norm"][0], a["ffn2_norm"][0], a["ffn1_norm"][1], a["mix_norm"][1],
             a["ffn2_norm"][1], a["kv_norm"]]
    gains = np.concatenate([g.reshape(DT, P).T for g in norms], axis=1)
    ins = [a["ffn1_w_in"][0], a["ffn2_w_in"][0], a["ffn1_w_in"][1], a["ffn2_w_in"][1]]
    w_in = np.concatenate([w.reshape(2, 4, P, 2, GROUPS, 2, P).transpose(4, 0, 2, 1, 3, 5, 6).reshape(-1, P, UNIT)
                           for w in ins])
    outs = [a["ffn1_w_out"][0], a["ffn2_w_out"][0], a["ffn1_w_out"][1], a["ffn2_w_out"][1]]
    w_out = np.concatenate([w.reshape(2, FT // 2, P, DT, P).transpose(3, 0, 2, 1, 4).reshape(-1, P, OUT_UNIT)
                            for w in outs])
    wr = a["ret_w_in"][0]
    qk = [wr[:, j * HEADS_R * DK:(j + 1) * HEADS_R * DK].reshape(DT, P, HEADS_R, P, 2).transpose(2, 1, 0, 4, 3)
          .reshape(HEADS_R, 1, P, UNIT) for j in range(2)]
    v, g = (wr[:, 2 * HEADS_R * DK + j * HEADS_R * DV:][:, :HEADS_R * DV] for j in range(2))
    v = v.reshape(2, 4, P, HEADS_R, DV).transpose(3, 0, 2, 1, 4).reshape(HEADS_R, 2, P, UNIT)
    g = g.reshape(DT, P, HEADS_R, 2, 2, P).transpose(2, 3, 1, 0, 4, 5).reshape(HEADS_R, 2, P, UNIT)
    w_ret = np.concatenate([qk[0], qk[1], v, g], axis=1).reshape(-1, P, UNIT)
    w_ret_out = a["ret_w_out"][0].reshape(YT, P, DT, P).transpose(2, 1, 0, 3).reshape(-1, P, UNIT)
    w_kv = a["kv_w"].reshape(DT, P, 2 * KVH * HD).transpose(1, 0, 2).reshape(1, P, UNIT)
    w_q = a["attn_w_q"][0].reshape(2, 4, P, 2, 512).transpose(3, 0, 2, 1, 4).reshape(-1, P, UNIT)
    w_o = a["attn_w_o"][0].reshape(2, 4, P, 2, 4, P).transpose(3, 0, 2, 4, 1, 5).reshape(-1, P, UNIT)
    rot, decay, rope, mask, ident = constants()
    swapped = [(n, np.concatenate([n[HD // 2:], n[:HD // 2]])) for n in (a["q_norm"][0], a["k_norm"])]
    head_gains = np.broadcast_to(np.stack([np.stack(s) for s in swapped])[None], (P, 2, 2, HD))
    sinks = np.broadcast_to(a["attn_sinks"][0][None], (P, HEADS_Q))

    arrays = dict(x_t=x_t, gains=gains, w_in=w_in, w_out=w_out, w_ret=w_ret, w_ret_out=w_ret_out, w_kv=w_kv,
                  w_q=w_q, w_o=w_o, rot=rot, decay=decay, rope=rope, head_gains=head_gains, mask=mask, sinks=sinks,
                  ident=ident)
    nc = bacc.Bacc("TRN2", target_bir_lowering=False, num_devices=1)
    feeds, args = {}, []
    for name, arr in arrays.items():
        arr = np.ascontiguousarray(arr)
        feeds[f"{name}_dram"] = arr
        args.append(nc.dram_tensor(f"{name}_dram", arr.shape, mybir.dt.from_np(arr.dtype), kind="ExternalInput").ap())
    out = nc.dram_tensor("out_dram", (P, DT, T), F32, kind="ExternalOutput").ap()
    trunk(nc, *args, out)
    r = run_bass_kernel_spmd(nc, [feeds], core_ids=[0])
    got = r.results[0]["out_dram"]
    return np.ascontiguousarray(got.transpose(2, 1, 0).reshape(1, T, D))
```

```python
import numpy as np

import concourse.bass as bass
from concourse import mybir

F32 = mybir.dt.float32
F32R = mybir.dt.float32r
I32 = mybir.dt.int32
ALU = mybir.AluOpType
ACT = mybir.ActivationFunctionType
AX = mybir.AxisListType
ds = bass.ds

P = 128
T = 256
D = 1024
DT = D // P
F = ((8 * D // 3) + 255) // 256 * 256
FT = F // P
GROUPS = FT // 2
EPS = 1e-6

HEADS_R, DK, DV = 4, 256, 512
YT = HEADS_R * DV // P
HEADS_Q, HD, KVH = 16, 64, 2
CH = 8
NEG = -1e30

SOFTMAXES = [(0, 0, 0, CH), (0, 1, 0, CH), (1, 0, 0, CH), (1, 1, 0, CH // 2), (1, 1, CH // 2, CH // 2)]
PIECES = [hs * (1 + b) // 4 for _, b, _, hs in SOFTMAXES]
SCALED_BY_ACT = 1

WARM_UP = 9
SLOTS = 4
UNIT = 2048
OUT_UNIT = FT // 2 * P

PHASES = [("in", 0, 22), ("out", 0, 16), ("ret", 0, 24), ("ret_out", 0, 8), ("in", 1, 22), ("out", 1, 16),
          ("in", 2, 22), ("kv", 0, 1), ("out", 2, 16), ("wq", 0, 4), ("wo", 0, 4), ("in", 3, 22), ("out", 3, 16)]
FIRST, _n = {}, 0
for _kind, _k, _units in PHASES:
    FIRST[_kind, _k] = _n
    _n += _units
UNITS = _n


def columns(u):
    for kind, k, n in PHASES:
        if FIRST[kind, k] <= u < FIRST[kind, k] + n:
            return OUT_UNIT if kind == "out" else UNIT
    return 0


NORMS = 6
KV_GAIN = 6
FFN_NORM = (0, 2, 3, 5)
RET, ATT = 1, 4
HEAD_SUMS = HEADS_R
CREDIT = 2


def sums_before(m):
    return m + (HEAD_SUMS if m > RET else 0)


def added_for(m):
    return DT * (m + 1) + (HEAD_SUMS if m > RET else 0)


class Chain:

    def __init__(self, eng, sem):
        self.eng, self.sem, self.n, self.i, self.per = eng, sem, 0, 0, 0

    def step(self, ins):
        ins.then_inc(self.sem, 1)
        self.n += 1
        self.eng.wait_ge(self.sem, self.n + self.per * self.i)

    def enter(self, i, per):
        self.i, self.per, self.start = i, per, self.n

    def leave(self, times):
        assert self.n - self.start == self.per, (self.n - self.start, self.per)
        self.n = self.start + self.per * times
        self.i = self.per = 0


def trunk(nc, x_t, gains, w_in, w_out, w_ret, w_ret_out, w_kv, w_q, w_o, rot, decay, rope, head_gains,
          mask_c, sinks_c, ident_c, out):
    def at(name, shape, dtype, offset):
        return nc.alloc_sbuf_tensor_at(name, shape, dtype, offset=offset)

    base = 16512
    stage = at("stage", [P, SLOTS, UNIT], F32, base)
    w_hi = at("w_hi", [P, SLOTS, UNIT], F32R, base + 32768)
    w_lo = at("w_lo", [P, SLOTS, UNIT], F32R, base + 65536)
    x = at("x", [P, DT, T], F32, base + 98304)
    h = at("h", [P, DT, 2 * T], F32R, base + 106496)
    big = base + 122880
    act_t = at("act_t", [P, FT, 2 * T], F32R, big)
    y_t = at("y_t", [P, YT, 2 * T], F32R, big)
    q_rot = at("q_rot", [P, 2, T], F32, big + 32768)
    k_rot = at("k_rot", [P, 2, T], F32, big + 34816)
    v_nat = at("v_nat", [P, 2, DV], F32, big + 36864)
    gate = at("gate", [P, 4, T], F32, big + 40960)
    q_nat = at("q_nat", [P, 2, 512], F32, big)
    q_a = at("q_a", [P, 2, 512], F32, big + 4096)
    q_b = at("q_b", [P, 2, 512], F32, big + 8192)
    q_sq = at("q_sq", [P, 2, 512], F32, big + 40960)
    q_t = at("q_t", [P, 4, T], F32, big + 12288)
    s_own = [at(f"s_own{c}", [P, CH, P], F32, (big + 16384, base + 106496)[c]) for c in range(2)]
    s_two = [at(f"s_two{c}", [P, CH, 2 * P], F32, (big + 20480, base + 110592)[c]) for c in range(2)]
    pt_own = at("pt_own", [P, CH, 1, P], F32, big + 28672)
    pt_two = at("pt_two", [P, CH, 2, P], F32, big + 32768)
    aux = big + 45056
    ret_cs = at("ret_cs", [P, 2, T], F32, aux)
    q_cs = at("q_cs", [P, 2, T], F32, aux + 2048)
    decay_s = at("decay_s", [P, HEADS_R, T], F32, aux + 4096)
    s_mask = at("s_mask", [P, 384], F32, aux + 8192)
    r_head = at("r_head", [P, T], F32, aux + 9728)
    rot_a = at("rot_a", [P, 2, T], F32, aux + 10752)
    rot_b = at("rot_b", [P, 2, T], F32, aux + 12800)
    h_kv = at("h_kv", [P, DT, 2 * T], F32R, aux)
    kv_nat = at("kv_nat", [P, 2, 2 * KVH * HD], F32, aux)
    k_a = at("k_a", [P, 2, KVH, HD], F32, aux + 2048)
    k_b = at("k_b", [P, 2, KVH, HD], F32, aux + 3072)
    k_pad = at("k_pad", [P, 2, KVH, 2, P], F32, aux + 4096)
    o_t = at("o_t", [P, DT, 2 * T], F32R, aux)
    misc = aux + 16384
    kz = at("kz", [P, KVH, 2, T], F32, misc)
    vz = at("vz", [P, KVH, 2, 2, P], F32, misc + 4096)
    y_f = at("y_f", [P, 4, T], F32, misc)
    y_sq = at("y_sq", [P, 4, T], F32, misc + 4096)
    rope_raw = at("rope_raw", [P, 2, 2, HD], F32, misc)
    gain_raw = at("gain_raw", [P, 2, 2, HD], F32, misc + 1024)
    tmp = at("tmp", [P, 2, 1024], F32, misc + 8192)
    tables = at("tables", [P, 2, 2, 2, HD], F32, misc + 16384)
    mask = at("mask", [P, 2 * P], F32, misc + 18432)
    ident = at("ident", [P, P], F32, misc + 19456)
    ones = at("ones", [P, P], F32, misc + 19968)
    r_row = at("r_row", [P, T], F32, misc + 20480)
    n_v = at("n_v", [P, T], F32, misc + 21504)
    n_t = at("n_t", [P, T], F32, misc + 22528)
    sq_sum = at("sq_sum", [P, T], F32, misc + 23552)
    sq = at("sq", [P, T], F32, misc + 24576)
    gain = at("gain", [P, (NORMS + 1) * DT], F32, misc + 25600)
    sinks = at("sinks", [P, HEADS_Q], F32, misc + 25824)
    r_col = at("r_col", [P, 4], F32, misc + 25888)
    col_v = at("col_v", [P, 4], F32, misc + 25920)
    col_t = at("col_t", [P, 4], F32, misc + 25952)
    hs = [at(f"hs{j}", [P, 2 * CH], F32, misc + 25984 + 64 * j) for j in range(4)]
    sm = at("sm", [P, len(SOFTMAXES), 5, CH], F32, misc + 26240)

    ps = nc.alloc_psum_tensor("ps", [P, 8, 512], F32)
    SUM = 7

    sem = nc.alloc_semaphore
    landed = [sem(f"landed{s}") for s in range(SLOTS)]
    hi_ready, lo_ready = sem("hi_ready"), sem("lo_ready")
    used = sem("used")
    x_loaded = [sem(f"x_loaded{j}") for j in range(4)]
    first_landed = [sem(f"first_landed{j}") for j in range(3)]
    first_hi, first_lo = sem("first_hi"), sem("first_lo")
    half_landed, half_hi, half_lo = sem("half_landed"), sem("half_hi"), sem("half_lo")
    gains_loaded, rot_loaded = sem("gains_loaded"), sem("rot_loaded")
    rope_loaded, mask_loaded = sem("rope_loaded"), sem("mask_loaded")
    ones_ready, zeroed, tables_ready = sem("ones_ready"), sem("zeroed"), sem("tables_ready")
    x_squared = sem("x_squared")
    sq_done, sum_added = sem("sq_done"), sem("sum_added")
    sum_done, sum_read, r_ready = sem("sum_done"), sem("sum_read"), sem("r_ready")
    h_hi, h_lo = sem("h_hi"), sem("h_lo")
    in_lo_half, in_free = sem("in_lo_half"), sem("in_free")
    in_scaled, in_silu, in_prod, in_hi = sem("in_scaled"), sem("in_silu"), sem("in_prod"), sem("in_hi")
    a_ready = sem("a_ready")
    tile_done, out_lo_half, x_done = sem("tile_done"), sem("out_lo_half"), sem("x_done")
    pair_lo_half, pair_free = sem("pair_lo_half"), sem("pair_free")
    rot_ready, v_copied = sem("rot_ready"), sem("v_copied")
    score_done, masked, pv_done = sem("score_done"), sem("masked"), sem("pv_done")
    g_scaled, g_silu = sem("g_scaled"), sem("g_silu")
    y_squared, y_half = sem("y_squared"), sem("y_half")
    y_done, y_hi, y_lo = sem("y_done"), sem("y_hi"), sem("y_lo")
    kvh_hi, kvh_lo, kv_copied = sem("kvh_hi"), sem("kvh_lo"), sem("kv_copied")
    vz_ready, kp_ready, kzt_done, kz_ready = sem("vz_ready"), sem("kp_ready"), sem("kzt_done"), sem("kz_ready")
    kp_zeroed = sem("kp_zeroed")
    q_squared, rq_ready = sem("q_squared"), sem("rq_ready")
    q_copied, q_roped, qt_done, qt_ready = sem("q_copied"), sem("q_roped"), sem("qt_done"), sem("qt_ready")
    s_done, s_read, max_ready, exp_done, p_ready = (sem("s_done"), sem("s_read"), sem("max_ready"),
                                                    sem("exp_done"), sem("p_ready"))
    sums_ready, p_scaled = sem("sums_ready"), sem("p_scaled")
    pt_done, pt_ready, o_done, o_hi, o_lo = sem("pt_done"), sem("pt_ready"), sem("o_done"), sem("o_hi"), sem("o_lo")
    dve_chain, pool_chain, act_chain = sem("dve_chain"), sem("pool_chain"), sem("act_chain")
    stored = sem("stored")

    def halves(banks):
        return ps[:, banks, 0:T], ps[:, banks, T:2 * T]

    def same(ap, n):
        return ap.rearrange("p (a c) -> p a c", a=1).broadcast_to([P, n, ap.shape[1]])

    with nc.Block() as block:
        @block.sync
        def _(sp):
            def load(src, u, j, i=0):
                if not isinstance(i, int) or u >= SLOTS:
                    sp.wait_ge(lo_ready, u - SLOTS + 1 + 4 * i)
                n = src.shape[2]
                sp.dma_start(stage[:, u % SLOTS, 0:n].rearrange("p (a n) -> p a n", a=1),
                             src[ds(j + 4 * i, 1), :, :].rearrange("a p n -> p a n")).then_inc(landed[u % SLOTS], 16)

            sources = {"in": w_in, "out": w_out, "ret": w_ret, "ret_out": w_ret_out, "kv": w_kv, "wq": w_q, "wo": w_o}
            for kind, k, n in PHASES:
                u, j = FIRST[kind, k], k * n
                peeled = SLOTS if u == 0 else 0
                if peeled:
                    sp.dma_start(gain[:], gains).then_inc(gains_loaded, 16)
                    for q in range(4):
                        cols = slice(q * UNIT // 4, (q + 1) * UNIT // 4)
                        sp.dma_start(stage[:, 0, cols], w_in[0, :, cols]).then_inc(
                            first_landed[q] if q < 3 else landed[0], 16)
                        sp.dma_start(x[:, 2 * q:2 * q + 2, :], x_t[:, 2 * q:2 * q + 2, :]).then_inc(x_loaded[q], 16)
                    for q in range(2):
                        cols = slice(q * UNIT // 2, (q + 1) * UNIT // 2)
                        sp.dma_start(stage[:, 1, cols], w_in[1, :, cols]).then_inc(
                            landed[1] if q else half_landed, 16)
                for e in range(2, peeled):
                    load(sources[kind], u + e, j + e)
                if peeled:
                    sp.dma_start(rope_raw[:], rope).then_inc(rope_loaded, 16)
                    sp.dma_start(gain_raw[:], head_gains).then_inc(rope_loaded, 16)
                    sp.dma_start(ret_cs[:], rot).then_inc(rot_loaded, 16)
                    sp.dma_start(decay_s[:], decay).then_inc(rot_loaded, 16)
                    sp.dma_start(mask[:], mask_c).then_inc(mask_loaded, 16)
                    sp.dma_start(sinks[:], sinks_c).then_inc(mask_loaded, 16)
                    sp.dma_start(ident[:], ident_c).then_inc(mask_loaded, 16)
                rounds = (n - peeled) // SLOTS
                if rounds > 1:
                    with sp.Fori(0, rounds) as i:
                        for e in range(SLOTS):
                            load(sources[kind], u + peeled + e, j + peeled + e, i)
                    peeled += rounds * SLOTS
                for e in range(peeled, n):
                    load(sources[kind], u + e, j + e)
            with sp.Fori(0, DT) as d:
                sp.wait_ge(x_done, CREDIT + DT * (NORMS - 1) + 1 + d)
                sp.dma_start(out[:, ds(d, 1), :], x[:, ds(d, 1), :]).then_inc(stored, 16)
            sp.wait_ge(stored, 16 * DT)

        @block.scalar
        def _(act):
            def split(u, i=0):
                n, s = columns(u), u % SLOTS
                if not n:
                    return
                if u >= SLOTS:
                    act.wait_ge(used, u - SLOTS + 1 + 4 * i)
                act.wait_ge(landed[s], 16 * (u // SLOTS + 1) + 16 * i)
                nc.scalar.activation(w_hi[:, s, 0:n], stage[:, s, 0:n], ACT.Copy).then_inc(hi_ready, 1)

            def h_hi_tile(m, d, i=0, per=0):
                if m:
                    act.wait_ge(x_done, CREDIT + DT * (m - 1) + d + 1 + per * i)
                else:
                    act.wait_ge(x_loaded[d // 2], 16)
                act.wait_ge(gains_loaded, 16)
                nc.scalar.activation(h[:, ds(d + per * i, 1), 0:T], x[:, ds(d + per * i, 1), :], ACT.Copy,
                                     scale=gain[:, ds(m * DT + d + per * i, 1)]).then_inc(h_hi, 1)

            def in_evac(f, g, i=0):
                u, c = FIRST["in", f] + 2 * g, GROUPS * f + g + 1 + 2 * i
                if g == GROUPS - 1:
                    split(u + 4)
                act.wait_ge(used, u + 2 + 4 * i)
                act.wait_ge(a_ready, c)
                t = tmp[:, g % 2, :].rearrange("p (o n) -> p o n", o=4)
                nc.scalar.activation(t, ps[:, 4 * (g % 2):4 * (g % 2) + 4, T:2 * T], ACT.Copy).then_inc(in_lo_half, 1)
                if g < GROUPS - 1:
                    split(u + 4, i)
                act.wait_ge(in_scaled, c)
                nc.scalar.activation(tmp[:, g % 2, 0:512], tmp[:, g % 2, 0:512], ACT.Silu).then_inc(in_silu, 1)
                split(u + 5, i)

            def out_evac(n, d, done, units, scale, i=0, per=0, bank=None):
                c = DT * n + d + 1 + per * i
                bank = 4 + d % 2 if bank is None else bank
                early = units[:1] if n in (RET, ATT) and d == 0 else ()
                for u in early:
                    split(u)
                if done:
                    act.wait_ge(used, done + 4 * i)
                else:
                    act.wait_ge(tile_done, (1, 2, 3, 0, 4, 0, 5)[d])
                act.wait_ge(x_done, c)
                nc.scalar.activation(tmp[:, d % 2, 0:T], ps[:, bank, T:2 * T], ACT.Copy,
                                     scale=scale).then_inc(out_lo_half, 1)
                first = units[len(early):1] if d < DT - 2 else ()
                for u in first:
                    split(u, i)
                if n + 1 < NORMS:
                    h_hi_tile(n + 1, d, i, per)
                for u in units[len(early) + len(first):]:
                    split(u, i)

            def ffn(f):
                m, u = FFN_NORM[f], FIRST["in", f]
                in_evac(f, 0)
                with act.Fori(0, 4) as i:
                    in_evac(f, 1, i)
                    in_evac(f, 2, i)
                if f == 2:
                    for d in range(DT):
                        nc.scalar.activation(h_kv[:, d, 0:T], x[:, d, :], ACT.Copy,
                                             scale=gain[:, KV_GAIN * DT + d:KV_GAIN * DT + d + 1]).then_inc(kvh_hi, 1)
                in_evac(f, 9)
                in_evac(f, 10)
                if f == 2:
                    act.wait_ge(used, FIRST["kv", 0] + 1)
                    act.wait_ge(r_ready, 1)
                    for t in range(2):
                        nc.scalar.activation(kv_nat[:, t, :], ps[:, 6 + t, 0:2 * KVH * HD], ACT.Copy,
                                             scale=r_col[:, 2 * t:2 * t + 1]).then_inc(kv_copied, 1)
                    split(FIRST["kv", 0] + 4)
                u = FIRST["out", f]
                with act.Fori(0, 3) as i:
                    out_evac(m, 0, u + 2, (u + 4, u + 5), 0.5, i, 2)
                    out_evac(m, 1, u + 4, (u + 6, u + 7), 0.5, i, 2)
                out_evac(m, 6, u + 14, (u + 16, u + 17), 0.5)
                out_evac(m, 7, u + 16, (u + 18, u + 19), 0.5)

            def ret_head(c):
                u = FIRST["ret", 0] + 6 * c

                def lo_half(j):
                    act.wait_ge(used, u + (1, 2, 5, 6)[j])
                    b = (0, 2, 2, 0)[j]
                    if j >= 2:
                        act.wait_ge(rot_ready, 2 * c + j - 1)
                    t = tmp[:, j % 2, 0:512].rearrange("p (a n) -> p a n", a=2)
                    nc.scalar.activation(t, ps[:, b:b + 2, T:2 * T], ACT.Copy).then_inc(pair_lo_half, 1)

                def silu(j):
                    act.wait_ge(g_scaled, 2 * c + j - 1)
                    act.wait_ge(y_done, c + 1)
                    t = tmp[:, j % 2, 0:512].rearrange("p (a n) -> p a n", a=2)
                    nc.scalar.activation(gate[:, 2 * (j - 2):2 * (j - 2) + 2, :], t, ACT.Silu).then_inc(g_silu, 1)

                lo_half(0)
                split(u + 4)
                lo_half(1)
                split(u + 5)
                if c:
                    store_y(c - 1)
                split(u + 6)
                act.wait_ge(used, u + 4)
                nc.scalar.activation(v_nat[:], ps[:, 0:2, :], ACT.Copy).then_inc(v_copied, 1)
                split(u + 7)
                lo_half(2)
                split(u + 8)
                silu(2)
                lo_half(3)
                split(u + 9)
                silu(3)
                act.wait_ge(pv_done, c + 1)
                act.wait_ge(sum_added, added_for(RET) + c)
                nc.scalar.activation(y_sq[:].rearrange("p (b a) n -> p b (a n)", b=2), ps[:, 5:7, :],
                                     ACT.Square).then_inc(y_squared, 1)

            def first_squares(k):
                act.wait_ge(x_loaded[2 + k], 16)
                nc.scalar.activation(y_sq[:, 2 * k:2 * k + 2, :], x[:, 4 + 2 * k:6 + 2 * k, :],
                                     ACT.Square).then_inc(x_squared, 1)

            def store_y(c):
                act.wait_ge(y_done, c + 2)
                nc.scalar.activation(y_t[:, 4 * c:4 * c + 4, 0:T], y_f[:], ACT.Copy).then_inc(y_hi, 1)

            def attention():
                u = FIRST["wq", 0]
                for c in range(2):
                    act.wait_ge(used, u + 2 * c + 2)
                    if c == 0:
                        act.wait_ge(r_ready, 2)
                    else:
                        act.wait_ge(q_roped, 1)
                        act.wait_ge(rq_ready, 1)
                    for t in range(2):
                        nc.scalar.activation(q_nat[:, t, :], ps[:, 2 * c + t, :], ACT.Copy,
                                             scale=r_col[:, 2 * t:2 * t + 1]).then_inc(q_copied, 1)
                    act.wait_ge(q_copied, 2 * c + 2)
                    nc.scalar.activation(q_sq[:], q_nat[:], ACT.Square).then_inc(q_squared, 1)
                    if c == 0:
                        split(u + 4)
                        act.wait_ge(kzt_done, 1)
                        for t in range(2):
                            nc.scalar.activation(
                                kz[:, :, :, t * P:(t + 1) * P],
                                ps[:, 4 + t, :].rearrange("p (g v n) -> p g v n", g=KVH, v=2),
                                ACT.Copy).then_inc(kz_ready, 1)
                        heads_to_rows(c)
                        split(u + 5)
                    else:
                        split(u + 6)
                        exps(0)
                        heads_to_rows(c)
                exps(1)
                split(u + 7)
                rows_of_p(0)
                scaled_p(SCALED_BY_ACT)
                rows_of_p(1)
                exps(2)
                output_hi(0)
                output_hi(1)
                exps(3)
                exps(4)
                rows_of_p(2)
                rows_of_p(3)
                output_hi(2)
                rows_of_p(4)
                output_hi(3)
                u = FIRST["wo", 0]
                for d in range(DT):
                    out_evac(ATT, d, {3: u + 2, 5: u + 3, 7: u + 4}.get(d),
                             {0: (u + 4,), 5: (u + 5,), 7: (u + 6, u + 7)}.get(d, ()), 1.0, bank=d)

            def heads_to_rows(c):
                act.wait_ge(qt_done, c + 1)
                if c:
                    act.wait_ge(s_done, 2)
                nc.scalar.activation(q_t[:].rearrange("p (b a) n -> p b (a n)", b=2), ps[:, 4:6, :],
                                     ACT.Copy).then_inc(qt_ready, 1)

            def exps(e):
                c, b, h0, n = SOFTMAXES[e]
                s = (s_two if b else s_own)[c]
                act.wait_ge(max_ready, e + 1)
                for j in range(h0, h0 + n):
                    nc.scalar.activation(s[:, j, :], s[:, j, :], ACT.Exp, bias=sm[:, e, 1, j:j + 1],
                                         accum_out=sm[:, e, 3, j:j + 1])
                nc.scalar.activation(sm[:, e, 2, h0:h0 + n], sm[:, e, 2, h0:h0 + n], ACT.Exp).then_inc(exp_done, 1)

            def scaled_p(e):
                c, b, h0, n = SOFTMAXES[e]
                s = (s_two if b else s_own)[c]
                act.wait_ge(sums_ready, 1)
                for j in range(h0, h0 + n):
                    ins = nc.scalar.activation(s[:, j, :], s[:, j, :], ACT.Copy, scale=sm[:, e, 4, j:j + 1])
                ins.then_inc(p_scaled, 1)

            def rows_of_p(e):
                c, b, h0, n = SOFTMAXES[e]
                pt = pt_two if b else pt_own
                if c:
                    act.wait_ge(o_done, 1 + b)
                heads = 4 // (1 + b)
                for j in range(PIECES[e]):
                    piece = sum(PIECES[:e]) + j
                    act.wait_ge(pt_done, piece + 1)
                    nc.scalar.activation(
                        pt[:, h0 + heads * j:h0 + heads * (j + 1), :, :],
                        ps[:, 4 + piece % 2, :].rearrange("p (a k n) -> p a k n", a=heads, n=P),
                        ACT.Copy).then_inc(pt_ready, 1)

            def output_hi(e):
                b, c = e % 2, e // 2
                act.wait_ge(o_done, e + 1)
                nc.scalar.activation(o_t[:, 4 * c:4 * c + 4, b * P:(b + 1) * P],
                                     ps[:, 6 + b, :].rearrange("p (a n) -> p a n", a=4), ACT.Copy).then_inc(o_hi, 1)

            for d in range(DT):
                if d < 4:
                    act.wait_ge(first_landed[d] if d < 3 else landed[0], 16)
                    cols = slice(d * UNIT // 4, (d + 1) * UNIT // 4)
                    nc.scalar.activation(w_hi[:, 0, cols], stage[:, 0, cols], ACT.Copy).then_inc(
                        first_hi if d < 3 else hi_ready, 1)
                h_hi_tile(0, d)
                if d == 5:
                    first_squares(0)
            for q in range(2):
                act.wait_ge(landed[1] if q else half_landed, 16)
                cols = slice(q * UNIT // 2, (q + 1) * UNIT // 2)
                nc.scalar.activation(w_hi[:, 1, cols], stage[:, 1, cols], ACT.Copy).then_inc(
                    hi_ready if q else half_hi, 1)
            first_squares(1)
            for u in range(2, 4):
                split(u)
            ffn(0)
            for c in range(HEADS_R):
                ret_head(c)
            store_y(HEADS_R - 1)
            u = FIRST["ret_out", 0]
            for d in range(DT):
                out_evac(RET, d, u + d + 1, (u + 4 + d,), 1.0, bank=d)
            ffn(1)
            ffn(2)
            attention()
            ffn(3)

        @block.vector
        def _(dve):
            chain = Chain(dve, dve_chain)

            def split(u, i=0, per=4):
                n, s = columns(u), u % SLOTS
                if not n:
                    return
                dve.wait_ge(hi_ready, u + 1 + per * i)
                nc.vector.tensor_tensor(w_lo[:, s, 0:n], stage[:, s, 0:n], w_hi[:, s, 0:n].bitcast(F32),
                                        ALU.subtract).then_inc(lo_ready, 1)

            def rsqrt(v, t, y):
                chain.step(nc.vector.tensor_scalar(t.bitcast(I32), v.bitcast(I32), 1, None, ALU.logical_shift_right))
                chain.step(nc.vector.tensor_scalar(y.bitcast(I32), t.bitcast(I32), -1.0, float(0x5F3759DF),
                                                   ALU.mult, ALU.add))
                for _ in range(3):
                    chain.step(nc.vector.tensor_tensor(t, y, y, ALU.mult))
                    chain.step(nc.vector.scalar_tensor_tensor(t, t, -0.5, v, ALU.mult, ALU.mult))
                    chain.step(nc.vector.scalar_tensor_tensor(y, t, 1.5, y, ALU.add, ALU.mult))

            def token_sums(m):
                dve.wait_ge(sum_done, sums_before(m) + 1)
                ins = nc.vector.tensor_scalar(n_v[:], ps[:, SUM, 0:T], 1.0 / D, EPS, ALU.mult, ALU.add)
                if m in (3, 4):
                    ins = nc.vector.tensor_scalar(col_v[:], ps[:, SUM, T:T + 4], 1.0 / D, EPS, ALU.mult, ALU.add)
                ins.then_inc(sum_read, 1)

            def token_scale(m):
                dve.wait_ge(sum_read, sums_before(m) + 1)
                if m != ATT:
                    rsqrt(n_v[:], n_t[:], r_row[:])
                if m in (3, 4):
                    rsqrt(col_v[:], col_t[:], r_col[:])
                    nc.vector.tensor_copy(col_t[:], r_col[:]).then_inc(r_ready, 1)

            def h_lo_tile(m, d, i=0, per=0):
                dve.wait_ge(h_hi, DT * m + d + 1 + per * i)
                nc.vector.scalar_tensor_tensor(
                    h[:, ds(d + per * i, 1), T:2 * T], x[:, ds(d + per * i, 1), :],
                    gain[:, ds(m * DT + d + per * i, 1)], h[:, ds(d + per * i, 1), 0:T].bitcast(F32),
                    ALU.mult, ALU.subtract).then_inc(h_lo, 1)

            def in_evac(f, g, i=0):
                u, n = FIRST["in", f] + 2 * g, GROUPS * f + g + 1 + 2 * i
                t = tmp[:, g % 2, :].rearrange("p (o n) -> p o n", o=4)
                if g == GROUPS - 1:
                    split(u + 4)
                dve.wait_ge(in_lo_half, n)
                nc.vector.tensor_tensor(t, ps[:, 4 * (g % 2):4 * (g % 2) + 4, 0:T], t, ALU.add).then_inc(in_free, 1)
                if g == 0 and f in (0, 3):
                    token_scale(FFN_NORM[f])
                dve.wait_ge(in_free, CREDIT + n)
                nc.vector.tensor_tensor(t, t, same(r_row[:], 4), ALU.mult).then_inc(in_scaled, 1)
                if g < GROUPS - 1:
                    split(u + 4, i)
                dve.wait_ge(in_silu, n)
                nc.vector.tensor_tensor(t[:, 0:2, :], t[:, 0:2, :], t[:, 2:4, :], ALU.mult).then_inc(in_prod, 1)
                dve.wait_ge(in_prod, n)
                hi = act_t[:, ds(2 * g + 4 * i, 2), 0:T]
                nc.vector.tensor_scalar(hi, t[:, 0:2, :], 1.0, None, ALU.mult).then_inc(in_hi, 1)
                dve.wait_ge(in_hi, n)
                nc.vector.tensor_tensor(act_t[:, ds(2 * g + 4 * i, 2), T:2 * T], t[:, 0:2, :], hi.bitcast(F32),
                                        ALU.subtract).then_inc(a_ready, 1)
                split(u + 5, i)

            def out_evac(n, d, units, scale, i=0, per=0, bank=None):
                c = DT * n + d + 1 + per * i
                bank = 4 + d % 2 if bank is None else bank
                early = units[:1] if n in (RET, ATT) and d == 0 else ()
                for u in early:
                    split(u)
                dve.wait_ge(out_lo_half, c)
                t = tmp[:, d % 2, 0:T]
                chain.step(nc.vector.scalar_tensor_tensor(t, ps[:, bank, 0:T], scale, t, ALU.mult, ALU.add))
                xd = x[:, ds(d + per * i, 1), :]
                nc.vector.tensor_tensor(xd, xd, t.rearrange("p (a n) -> p a n", a=1), ALU.add).then_inc(x_done, 1)
                first = units[len(early):1] if d < DT - 2 else ()
                for u in first:
                    split(u, i)
                if n + 1 < NORMS:
                    h_lo_tile(n + 1, d, i, per)
                for u in units[len(early) + len(first):]:
                    split(u, i)

            def ffn(f):
                m = FFN_NORM[f]
                token_sums(m)
                if f in (0, 3):
                    split(FIRST["in", f] + 3)
                else:
                    token_scale(m)
                in_evac(f, 0)
                with dve.Fori(0, 4) as i:
                    in_evac(f, 1, i)
                    in_evac(f, 2, i)
                if f == 2:
                    for d in range(DT):
                        dve.wait_ge(kvh_hi, d + 1)
                        nc.vector.scalar_tensor_tensor(
                            h_kv[:, d, T:2 * T], x[:, d, :], gain[:, KV_GAIN * DT + d:KV_GAIN * DT + d + 1],
                            h_kv[:, d, 0:T].bitcast(F32), ALU.mult, ALU.subtract).then_inc(kvh_lo, 1)
                in_evac(f, 9)
                in_evac(f, 10)
                if f == 2:
                    split(FIRST["kv", 0] + 4)
                    shared_k()
                u = FIRST["out", f]
                with dve.Fori(0, 3) as i:
                    chain.enter(i, 2)
                    out_evac(m, 0, (u + 4, u + 5), 0.5, i, 2)
                    out_evac(m, 1, (u + 6, u + 7), 0.5, i, 2)
                chain.leave(3)
                out_evac(m, 6, (u + 16, u + 17), 0.5)
                out_evac(m, 7, (u + 18, u + 19), 0.5)

            def rope_(src, a, b, n, which, t):
                cos, sin, half = same(tables[:, which, 0, t, :], n), tables[:, which, 1, t, :], HD // 2
                nc.vector.tensor_tensor(a, src, cos, ALU.mult)
                for k in range(2):
                    o, w = k * half, (1 - k) * half
                    ins = nc.vector.tensor_tensor(b[:, :, o:o + half], src[:, :, w:w + half],
                                                  same(sin[:, o:o + half], n), ALU.mult)
                chain.step(ins)
                return nc.vector.tensor_tensor(a, a, b, ALU.add)

            def per_head(ap, n):
                return ap.rearrange("p (g a) -> p g a", a=1).broadcast_to([P, n, HD])

            def shared_k():
                dve.wait_ge(kv_copied, 2)
                dve.wait_ge(tables_ready, 4)
                dve.wait_ge(kp_zeroed, 1)
                k = kv_nat[:, :, 0:KVH * HD].rearrange("p t (h e) -> p t h e", h=KVH)
                ss, sv, sr = (z[:, 0:2 * KVH] for z in hs[:3])
                chain.step(nc.vector.tensor_tensor(k_a[:], k, k, ALU.mult))
                chain.step(nc.vector.tensor_reduce(ss, k_a[:].rearrange("p t h e -> p (t h) e"), AX.X, ALU.add))
                chain.step(nc.vector.tensor_scalar(sv, ss, 1.0 / HD, EPS, ALU.mult, ALU.add))
                rsqrt(sv, ss, sr)
                for t in range(2):
                    chain.step(nc.vector.tensor_tensor(k[:, t], k[:, t], per_head(sr[:, KVH * t:KVH * (t + 1)], KVH),
                                                       ALU.mult))
                    chain.step(rope_(k[:, t], k_a[:, t], k_b[:, t], KVH, 1, t))
                for v in range(2):
                    ins = nc.vector.tensor_copy(k_pad[:, :, :, v, v * HD:(v + 1) * HD], k_a[:])
                ins.then_inc(kp_ready, 1)

            def q_rope(c):
                v4 = [z[:].rearrange("p t (h e) -> p t h e", h=CH) for z in (q_nat, q_a, q_b)]
                if c:
                    dve.wait_ge(qt_done, 1)
                dve.wait_ge(q_copied, 2 * c + 2)
                rope_(v4[0][:, 0], v4[1][:, 0], v4[2][:, 0], CH, 0, 0)
                rope_(v4[0][:, 1], v4[1][:, 1], v4[2][:, 1], CH, 0, 1).then_inc(q_roped, 1)

            def q_scale(c):
                ss, sv, sr = hs[0][:], hs[1][:], hs[2 + c][:]
                dve.wait_ge(q_squared, c + 1)
                chain.step(nc.vector.tensor_reduce(ss, q_sq[:].rearrange("p t (h e) -> p (t h) e", h=CH),
                                                   AX.X, ALU.add))
                chain.step(nc.vector.tensor_scalar(sv, ss, 1.0, EPS * HD, ALU.mult, ALU.add))
                rsqrt(sv, ss, sr)
                nc.vector.tensor_copy(sv, sr).then_inc(rq_ready, 1)

            def ret_head(c):
                u = FIRST["ret", 0] + 6 * c
                t2 = [tmp[:, j, 0:512].rearrange("p (a n) -> p a n", a=2) for j in range(2)]

                def add_halves(j):
                    dve.wait_ge(pair_lo_half, 4 * c + j + 1)
                    b = (0, 2, 2, 0)[j]
                    nc.vector.tensor_tensor(t2[j % 2], ps[:, b:b + 2, 0:T], t2[j % 2], ALU.add).then_inc(pair_free, 1)
                    dve.wait_ge(pair_free, 4 + 4 * c + j + 1)

                def rotate(j, dst, cs):
                    t = t2[j % 2]
                    nc.vector.tensor_tensor(rot_a[:], t, same(cs[:, 0, :], 2), ALU.mult)
                    nc.vector.tensor_tensor(rot_b[:, 0, :], t[:, 1, :], cs[:, 1, :], ALU.mult)
                    chain.step(nc.vector.tensor_tensor(rot_b[:, 1, :], t[:, 0, :], cs[:, 1, :], ALU.mult))
                    nc.vector.tensor_tensor(dst[:, 0, :], rot_a[:, 0, :], rot_b[:, 0, :], ALU.subtract)
                    nc.vector.tensor_tensor(dst[:, 1, :], rot_a[:, 1, :], rot_b[:, 1, :],
                                            ALU.add).then_inc(rot_ready, 1)
                    dve.wait_ge(rot_ready, 2 * c + j + 1)

                def scale_gate(j):
                    nc.vector.tensor_tensor(t2[j % 2], t2[j % 2], same(r_row[:], 2), ALU.mult).then_inc(g_scaled, 1)

                add_halves(0)
                if c == 0:
                    scaled_tables()
                rotate(0, q_rot, q_cs)
                split(u + 4)
                if c:
                    norm_y(c - 1)
                add_halves(1)
                rotate(1, k_rot, ret_cs)
                split(u + 5)
                if c:
                    store_y(c - 1)
                split(u + 6)
                split(u + 7)
                add_halves(2)
                scale_gate(2)
                dve.wait_ge(score_done, c + 1)
                nc.vector.tensor_tensor(s_mask[:, 0:T], ps[:, 4, 0:T], decay_s[:, c, :], ALU.mult)
                nc.vector.tensor_tensor(s_mask[:, T:T + P], ps[:, 4, T:T + P], decay_s[:, c, 0:P],
                                        ALU.mult).then_inc(masked, 1)
                split(u + 8)
                add_halves(3)
                scale_gate(3)
                split(u + 9)

            def norm_y(c):
                n = sums_before(RET) + 1 + c + 1
                dve.wait_ge(sum_done, n)
                nc.vector.tensor_scalar(n_v[:], ps[:, SUM, 0:T], 1.0 / DV, EPS, ALU.mult, ALU.add).then_inc(sum_read, 1)
                dve.wait_ge(sum_read, n)
                rsqrt(n_v[:], n_t[:], r_head[:])
                chain.step(nc.vector.tensor_tensor(y_f[:].rearrange("p (b a) n -> p b a n", b=2),
                                                   ps[:, 5:7, :].rearrange("p b (a n) -> p b a n", a=2),
                                                   r_head[:].rearrange("p (b a n) -> p b a n", b=1, a=1)
                                                   .broadcast_to([P, 2, 2, T]), ALU.mult))
                dve.wait_ge(g_silu, 2 * c + 2)
                nc.vector.tensor_tensor(y_f[:], y_f[:], gate[:], ALU.mult).then_inc(y_done, 1)
                dve.wait_ge(y_done, c + 2)

            def store_y(c):
                dve.wait_ge(y_hi, c + 1)
                nc.vector.tensor_tensor(y_t[:, 4 * c:4 * c + 4, T:2 * T], y_f[:],
                                        y_t[:, 4 * c:4 * c + 4, 0:T].bitcast(F32), ALU.subtract).then_inc(y_lo, 1)

            def scaled_tables():
                token_sums(RET)
                token_scale(RET)
                dve.wait_ge(rot_loaded, 32)
                r2 = same(r_row[:], 2)
                chain.step(nc.vector.tensor_tensor(q_cs[:], ret_cs[:], r2, ALU.mult))
                chain.step(nc.vector.scalar_tensor_tensor(ret_cs[:], q_cs[:], float(DK) ** -0.5, r2,
                                                          ALU.mult, ALU.mult))

            def retention():
                for c in range(HEADS_R):
                    ret_head(c)
                norm_y(HEADS_R - 1)
                store_y(HEADS_R - 1)
                u = FIRST["ret_out", 0]
                for d in range(DT):
                    out_evac(RET, d, (u + 4 + d,), 1.0, bank=d)

            def softmax_front(e):
                c, b, h0, n = SOFTMAXES[e]
                s = (s_two if b else s_own)[c]
                dve.wait_ge(s_done, e + 1)
                for j in range(h0, h0 + n):
                    if b:
                        scores, m_ = ps[:, j // 2, (j % 2) * T:(j % 2 + 1) * T], mask[:]
                    else:
                        scores, m_ = ps[:, 6 + j // 4, (j % 4) * P:(j % 4 + 1) * P], mask[:, P:2 * P]
                    ins = nc.vector.scalar_tensor_tensor(s[:, j, :], scores, hs[2 + c][:, CH * b + j:CH * b + j + 1],
                                                         m_, ALU.mult, ALU.add)
                ins.then_inc(s_read, 1)
                dve.wait_ge(s_read, e + 1)
                mx, neg, sk = (sm[:, e, k, h0:h0 + n] for k in range(3))
                sink = sinks[:, CH * c + h0:CH * c + h0 + n]
                chain.step(nc.vector.tensor_reduce(mx, s[:, h0:h0 + n, :], AX.X, ALU.max))
                chain.step(nc.vector.tensor_tensor(mx, mx, sink, ALU.max))
                nc.vector.tensor_scalar(neg, mx, -1.0, None, ALU.mult)
                nc.vector.tensor_tensor(sk, sink, mx, ALU.subtract).then_inc(max_ready, 1)

            def softmax_back(e):
                c, b, h0, n = SOFTMAXES[e]
                s = (s_two if b else s_own)[c][:, h0:h0 + n, :]
                dve.wait_ge(exp_done, e + 1)
                sk, den, rden = (sm[:, e, k, h0:h0 + n] for k in (2, 3, 4))
                chain.step(nc.vector.tensor_tensor(den, den, sk, ALU.add))
                ins = nc.vector.reciprocal(rden, den)
                if e == SCALED_BY_ACT:
                    ins.then_inc(sums_ready, 1)
                else:
                    chain.step(ins)
                    nc.vector.tensor_tensor(
                        s, s, rden.rearrange("p (g a) -> p g a", a=1).broadcast_to([P, n, P * (1 + b)]),
                        ALU.mult).then_inc(p_ready, 1)

            def out_lo(e):
                c, b = e // 2, e % 2
                dve.wait_ge(o_hi, e + 1)
                dst = o_t[:, 4 * c:4 * c + 4, :]
                nc.vector.tensor_tensor(dst[:, :, T + b * P:T + (b + 1) * P],
                                        ps[:, 6 + b, :].rearrange("p (a n) -> p a n", a=4),
                                        dst[:, :, b * P:(b + 1) * P].bitcast(F32), ALU.subtract).then_inc(o_lo, 1)

            def attention():
                token_sums(ATT)
                token_scale(ATT)
                dve.wait_ge(mask_loaded, 48)
                q_rope(0)
                q_scale(0)
                softmax_front(0)
                q_rope(1)
                softmax_front(1)
                softmax_back(0)
                q_scale(1)
                softmax_back(1)
                softmax_front(2)
                softmax_front(3)
                softmax_front(4)
                softmax_back(2)
                out_lo(0)
                out_lo(1)
                softmax_back(3)
                softmax_back(4)
                out_lo(2)
                out_lo(3)
                u = FIRST["wo", 0]
                dve.wait_ge(lo_ready, u + 4)
                for d in range(DT):
                    out_evac(ATT, d, {0: (u + 4,), 5: (u + 5,), 7: (u + 6,)}.get(d, ()), 1.0, bank=d)

            dve.sem_inc(in_free, CREDIT)
            dve.sem_inc(a_ready, CREDIT)
            dve.sem_inc(x_done, CREDIT)
            dve.sem_inc(pair_free, 4)
            dve.sem_inc(y_done, 1)
            nc.vector.memset(ones[:], 1.0).then_inc(ones_ready, 1)
            for d in range(DT):
                if d < 4:
                    if d < 3:
                        dve.wait_ge(first_hi, d + 1)
                    else:
                        dve.wait_ge(hi_ready, 1)
                    cols = slice(d * UNIT // 4, (d + 1) * UNIT // 4)
                    nc.vector.tensor_tensor(w_lo[:, 0, cols], stage[:, 0, cols], w_hi[:, 0, cols].bitcast(F32),
                                            ALU.subtract).then_inc(first_lo if d < 3 else lo_ready, 1)
                h_lo_tile(0, d)
            for q in range(2):
                if q:
                    dve.wait_ge(hi_ready, 2)
                else:
                    dve.wait_ge(half_hi, 1)
                cols = slice(q * UNIT // 2, (q + 1) * UNIT // 2)
                nc.vector.tensor_tensor(w_lo[:, 1, cols], stage[:, 1, cols], w_hi[:, 1, cols].bitcast(F32),
                                        ALU.subtract).then_inc(lo_ready if q else half_lo, 1)
            split(2)
            ffn(0)
            retention()
            ffn(1)
            ffn(2)
            attention()
            ffn(3)

        @block.gpsimd
        def _(pool):
            def square_sum(m):
                pool.wait_ge(sum_done, sums_before(m))
                pool.wait_ge(x_done, CREDIT + DT * (m - 1) + 1)
                nc.gpsimd.tensor_tensor(sq_sum[:], x[:, 0, :], x[:, 0, :], ALU.mult).then_inc(sum_added, 1)
                with pool.Fori(0, DT - 1) as i:
                    pool.wait_ge(sum_added, added_for(m) - DT + 1 + i)
                    pool.wait_ge(x_done, CREDIT + DT * (m - 1) + 2 + i)
                    pool.wait_ge(x_loaded[3], 16)
                    nc.gpsimd.tensor_tensor(sq[:].rearrange("p (a n) -> p a n", a=1), x[:, ds(i + 1, 1), :],
                                            x[:, ds(i + 1, 1), :], ALU.mult).then_inc(sq_done, 1)
                    pool.wait_ge(sq_done, 3 + (DT - 1) * (m - 1) + 1 + i)
                    nc.gpsimd.tensor_tensor(sq_sum[:], sq_sum[:], sq[:], ALU.add).then_inc(sum_added, 1)

            for d in range(DT):
                if d < 4:
                    pool.wait_ge(x_loaded[d // 2], 16)
                    nc.gpsimd.tensor_tensor(sq[:] if d else sq_sum[:], x[:, d, :], x[:, d, :],
                                            ALU.mult).then_inc(sq_done if d else sum_added, 1)
                if d:
                    if d < 4:
                        pool.wait_ge(sq_done, d)
                    else:
                        pool.wait_ge(x_squared, d // 2 - 1)
                    pool.wait_ge(sum_added, d)
                    nc.gpsimd.tensor_tensor(sq_sum[:], sq_sum[:], sq[:] if d < 4 else y_sq[:, d - 4, :],
                                            ALU.add).then_inc(sum_added, 1)
                    pool.wait_ge(sum_added, d + 1)
            pool.wait_ge(rope_loaded, 32)
            for w in range(2):
                for k in range(2):
                    nc.gpsimd.tensor_tensor(tables[:, w, k, :, :], rope_raw[:, k, :, :],
                                            same(gain_raw[:, w, k, :], 2), ALU.mult).then_inc(tables_ready, 1)
            pool.wait_ge(tables_ready, 4)
            square_sum(RET)
            ysf = y_sq[:].rearrange("p a n -> p (a n)")
            with pool.Fori(0, HEADS_R) as i:
                pool.wait_ge(y_squared, i + 1)
                nc.gpsimd.tensor_tensor(ysf[:, 0:512], ysf[:, 0:512], ysf[:, 512:1024], ALU.add).then_inc(y_half, 1)
                pool.wait_ge(y_half, i + 1)
                pool.wait_ge(sum_done, sums_before(RET) + 1 + i)
                nc.gpsimd.tensor_tensor(sq_sum[:], ysf[:, 0:T], ysf[:, T:2 * T], ALU.add).then_inc(sum_added, 1)
            square_sum(2)
            nc.gpsimd.memset(vz[:], 0.0).then_inc(zeroed, 1)
            square_sum(3)
            pool.wait_ge(kv_copied, 2)
            nc.gpsimd.memset(k_pad[:], 0.0).then_inc(kp_zeroed, 1)
            pool.wait_ge(zeroed, 1)
            v = kv_nat[:, :, KVH * HD:2 * KVH * HD].rearrange("p t (g e) -> p t g e", g=KVH)
            for t in range(2):
                for k in range(2):
                    nc.gpsimd.tensor_copy(vz[:, :, t, k, k * HD:(k + 1) * HD], v[:, t]).then_inc(vz_ready, 1)
            square_sum(ATT)
            for u in range(FIRST["wo", 0], FIRST["wo", 0] + 4):
                pool.wait_ge(hi_ready, u + 1)
                pool.wait_ge(lo_ready, u)
                nc.gpsimd.tensor_tensor(w_lo[:, u % SLOTS, :], stage[:, u % SLOTS, :],
                                        w_hi[:, u % SLOTS, :].bitcast(F32), ALU.subtract).then_inc(lo_ready, 1)
            square_sum(5)

        @block.tensor
        def _(pe):
            def matmul(out_, w, x_, start, stop):
                return nc.tensor.matmul(out_, w, x_, start=start, stop=stop)

            def weight_block(bank, slot, b, moving, first, last):
                cols = slice(b * P, (b + 1) * P)
                matmul(ps[:, bank, :], w_hi[:, slot, cols], moving, first, False)
                return matmul(ps[:, bank, 0:T], w_lo[:, slot, cols], moving[:, 0:T], False, last)

            def token_block(out_, slot, cols, acts, t, first, last):
                hi, lo = acts[:, t * P:(t + 1) * P], acts[:, T + t * P:T + (t + 1) * P]
                matmul(out_, hi, w_hi[:, slot, cols], first, False)
                matmul(out_, lo, w_hi[:, slot, cols], False, False)
                return matmul(out_, hi, w_lo[:, slot, cols], False, last)

            def norm_sum(m):
                pe.wait_ge(sum_added, added_for(m))
                last = matmul(ps[:, SUM, 0:T], ones[:], sq_sum[:], True, True)
                if m in (3, 4):
                    for t in range(2):
                        last = matmul(ps[:, SUM, T + 2 * t:T + 2 * t + 2], sq_sum[:, t * P:(t + 1) * P],
                                      ones[:, 0:2], True, True)
                last.then_inc(sum_done, 1)

            def in_group(f, g, i=0):
                m, u = FFN_NORM[f], FIRST["in", f] + 2 * g
                pe.wait_ge(in_free, GROUPS * f + g + 1 + 2 * i)
                if g == 0 and m - 1 in (RET, ATT):
                    pe.wait_ge(x_done, CREDIT + DT * (m - 1) + 4)
                if g == 1:
                    pe.wait_ge(sum_read, sums_before(m) + 1)
                for part in range(2):
                    if u + part > 1:
                        pe.wait_ge(lo_ready, u + part + 1 + 4 * i)
                    for k in range(4):
                        kt = 4 * part + k
                        if u + part == 0:
                            if k < 3:
                                pe.wait_ge(first_lo, k + 1)
                            else:
                                pe.wait_ge(lo_ready, 1)
                        if u + part == 1 and k in (0, 2):
                            if k:
                                pe.wait_ge(lo_ready, 2)
                            else:
                                pe.wait_ge(half_lo, 1)
                        if g == 0:
                            pe.wait_ge(h_lo, DT * m + kt + 1)
                        for o in range(4):
                            last = weight_block(4 * (g % 2) + o, (u + part) % SLOTS, 4 * k + o, h[:, kt, :],
                                                kt == 0, kt == DT - 1)
                        if g == 0 and kt == 5:
                            norm_sum(m)
                    if part == 0:
                        last.then_inc(used, 1)
                last.then_inc(used, 1)

            def ffn(f):
                m = FFN_NORM[f]
                in_group(f, 0)
                with pe.Fori(0, (GROUPS - 1) // 2) as i:
                    in_group(f, 1, i)
                    in_group(f, 2, i)
                if f == 2:
                    shared_kv()
                pe.wait_ge(in_free, CREDIT + GROUPS * f + GROUPS - 1)
                u0 = FIRST["out", f]
                with pe.Fori(0, DT // 2) as i:
                    for d in range(2):
                        pe.wait_ge(x_done, DT * m + d + 1 + 2 * i)
                        for part in range(2):
                            u = u0 + 2 * d + part
                            pe.wait_ge(lo_ready, u + 1 + 4 * i)
                            for b in range(FT // 2):
                                k = FT // 2 * part + b
                                if d == 0 and k % 2 == 0:
                                    if k in (0, 10, 18, 20):
                                        pe.wait_ge(a_ready, CREDIT + GROUPS * f + {0: 5, 10: 9, 18: 10, 20: 11}[k])
                                last = weight_block(4 + d, u % SLOTS, b, act_t[:, k, :], k == 0, k == FT - 1)
                            last.then_inc(used, 1)

            def shared_kv():
                u = FIRST["kv", 0]
                pe.wait_ge(in_free, CREDIT + GROUPS * 2 + GROUPS - 1)
                pe.wait_ge(kvh_lo, DT)
                pe.wait_ge(lo_ready, u + 1)
                for t in range(2):
                    for k in range(DT):
                        last = token_block(ps[:, 6 + t, 0:2 * KVH * HD], u % SLOTS, slice(256 * k, 256 * (k + 1)),
                                           h_kv[:, k, :], t, k == 0, k == DT - 1)
                last.then_inc(used, 1)

            def pair(u, banks, i):
                pe.wait_ge(lo_ready, u + 1 + 12 * i)
                for k in range(DT):
                    if u == FIRST["ret", 0]:
                        pe.wait_ge(h_lo, DT * RET + k + 1)
                    for o in range(2):
                        last = weight_block(banks + o, u % SLOTS, 2 * k + o, h[:, k, :], k == 0, k == DT - 1)
                last.then_inc(used, 1)

            def ret_head(hh, i):
                u, c = FIRST["ret", 0] + 6 * hh, hh + 2 * i
                pe.wait_ge(pair_free, 4 * c + 4)
                pair(u, 0, i)
                head_sum(c)
                pair(u + 1, 2, i)
                pe.wait_ge(pair_free, 4 + 4 * c + 1)
                for part in range(2):
                    pe.wait_ge(lo_ready, u + 3 + part + 12 * i)
                    for t in range(2):
                        for k in range(4):
                            kt = 4 * part + k
                            last = token_block(ps[:, t, :], (u + 2 + part) % SLOTS, slice(512 * k, 512 * (k + 1)),
                                               h[:, kt, :], t, kt == 0, kt == DT - 1)
                    last.then_inc(used, 1)
                pe.wait_ge(pair_free, 4 + 4 * c + 2)
                pair(u + 4, 2, i)
                pe.wait_ge(rot_ready, 2 * c + 2)
                for kb in range(2):
                    for e in range(2):
                        last = matmul(ps[:, 4, T * kb:T + P * kb], k_rot[:, e, kb * P:(kb + 1) * P],
                                      q_rot[:, e, kb * P:T], e == 0, e == 1)
                last.then_inc(score_done, 1)
                pe.wait_ge(v_copied, c + 1)
                pair(u + 5, 0, i)
                pe.wait_ge(masked, c + 1)
                pe.wait_ge(y_done, c + 1)
                for e in range(4):
                    o = ps[:, 5 + e // 2, T * (e % 2):T * (e % 2 + 1)]
                    matmul(o, v_nat[:, 0, e * P:(e + 1) * P], s_mask[:, 0:T], True, False)
                    last = matmul(o[:, P:T], v_nat[:, 1, e * P:(e + 1) * P], s_mask[:, T:T + P], False, True)
                last.then_inc(pv_done, 1)

            def head_sum(c):
                pe.wait_ge(sum_added, added_for(RET) + c)
                pe.wait_ge(sum_read, sums_before(RET) + c)
                matmul(ps[:, SUM, 0:T], ones[:], sq_sum[:], True, True).then_inc(sum_done, 1)

            def retention():
                with pe.Fori(0, 2) as i:
                    ret_head(0, i)
                    ret_head(1, i)
                u0 = FIRST["ret_out", 0]
                half = YT - YT // HEADS_R
                pe.wait_ge(pair_free, 4 + 4 * HEADS_R)
                pe.wait_ge(y_lo, HEADS_R - 1)
                for d in range(4):
                    pe.wait_ge(lo_ready, u0 + d + 1)
                    for k in range(half):
                        weight_block(d, (u0 + d) % SLOTS, k, y_t[:, k, :], k == 0, False)
                    if d == 0:
                        head_sum(HEADS_R)
                pe.wait_ge(y_lo, HEADS_R)
                for d in range(DT):
                    if d >= 4:
                        pe.wait_ge(lo_ready, u0 + d + 1)
                    for k in range(half if d < 4 else 0, YT):
                        last = weight_block(d, (u0 + d) % SLOTS, k, y_t[:, k, :], k == 0, k == YT - 1)
                    last.then_inc(used, 1)

            def q_unit(c, part, ks=range(4)):
                u = FIRST["wq", 0] + 2 * c + part
                pe.wait_ge(lo_ready, u + 1)
                for k in ks:
                    kt = 4 * part + k
                    if c == 0:
                        pe.wait_ge(h_lo, DT * ATT + kt + 1)
                    for t in range(2):
                        last = token_block(ps[:, 2 * c + t, :], u % SLOTS, slice(512 * k, 512 * (k + 1)),
                                           h[:, kt, :], t, kt == 0, kt == DT - 1)
                if k == 3:
                    last.then_inc(used, 1)

            def q_transposes(c):
                pe.wait_ge(q_roped, c + 1)
                if c:
                    pe.wait_ge(qt_ready, 1)
                else:
                    pe.wait_ge(kz_ready, 2)
                for p in range(4):
                    for t in range(2):
                        o = (p % 2) * T + t * P
                        last = nc.tensor.transpose(ps[:, 4 + p // 2, o:o + P], q_a[:, t, p * P:(p + 1) * P], ident[:])
                last.then_inc(qt_done, 1)

            def scores_own(c):
                pe.wait_ge(qt_ready, c + 1)
                if c:
                    pe.wait_ge(s_read, 1)
                else:
                    pe.wait_ge(sum_read, sums_before(ATT) + 1)
                for p in range(4):
                    last = matmul(ps[:, 6 + p // 2, (p % 2) * T:(p % 2) * T + T], q_t[:, p, 0:P],
                                  kz[:, c, :, 0:P], True, True)
                last.then_inc(s_done, 1)

            def scores_two(c):
                if c:
                    pe.wait_ge(s_read, 2)
                else:
                    pe.wait_ge(q_copied, 4)
                for p in range(4):
                    last = matmul(ps[:, p, :], q_t[:, p, P:T], kz[:, c, :, :], True, True)
                    if (c, 1, 0, 2 * (p + 1)) in SOFTMAXES:
                        last.then_inc(s_done, 1)
                if (c, 1, 0, CH) not in SOFTMAXES:
                    last.then_inc(s_done, 1)

            def transposed_p(e):
                c, b, h0, n = SOFTMAXES[e]
                s = (s_two if b else s_own)[c]
                if e == SCALED_BY_ACT:
                    pe.wait_ge(p_scaled, 1)
                else:
                    pe.wait_ge(p_ready, e + 1 - (e > SCALED_BY_ACT))
                for j in range(PIECES[e]):
                    piece = sum(PIECES[:e]) + j
                    if piece >= 2:
                        pe.wait_ge(pt_ready, piece - 1)
                    else:
                        pe.wait_ge(qt_ready, 2)
                    for q in range(4):
                        tile = 4 * j + q
                        head, kb = (tile // 2, tile % 2) if b else (tile, 0)
                        last = nc.tensor.transpose(ps[:, 4 + piece % 2, q * P:(q + 1) * P],
                                                   s[:, h0 + head, kb * P:(kb + 1) * P], ident[:])
                    last.then_inc(pt_done, 1)

            def values(e):
                c, b, h0, n = SOFTMAXES[e]
                pt = pt_two if b else pt_own
                pe.wait_ge(pt_ready, sum(PIECES[:e + 1]))
                if c:
                    pe.wait_ge(o_lo, 1 + b)
                else:
                    pe.wait_ge(s_read, 3)
                for p in range(h0 // 2, (h0 + n) // 2):
                    m = 0
                    for k in range(2):
                        for kb in range(1 + b):
                            last = matmul(ps[:, 6 + b, p * P:(p + 1) * P], vz[:, c, kb, k, :],
                                          pt[:, 2 * p + k, kb, :], m == 0, m == 2 * (1 + b) - 1)
                            m += 1
                if h0 + n == CH:
                    last.then_inc(o_done, 1)

            def wo_unit(j, part=range(4)):
                u = FIRST["wo", 0] + j
                pe.wait_ge(lo_ready, u + 1)
                tiles, kts = (range(4), range(4 * j, 4 * j + 4)) if j < 2 else (range(2 * j, 2 * j + 2), range(DT))
                for n, d in enumerate(tiles):
                    if n not in part:
                        continue
                    for k, kt in enumerate(kts):
                        last = weight_block(d, u % SLOTS, len(kts) * n + k, o_t[:, kt, :], kt == 0, kt == DT - 1)
                    if j and d != tiles[-1]:
                        last.then_inc(tile_done, 1)
                if d in part or j:
                    last.then_inc(used, 1)

            def attention():
                q_unit(0, 0)
                norm_sum(ATT)
                q_unit(0, 1)
                pe.wait_ge(kp_ready, 1)
                pe.wait_ge(mask_loaded, 48)
                for t in range(2):
                    for g in range(KVH):
                        for k in range(2):
                            o = (2 * g + k) * P
                            last = nc.tensor.transpose(ps[:, 4 + t, o:o + P], k_pad[:, t, g, k, :], ident[:])
                last.then_inc(kzt_done, 1)
                q_unit(1, 0)
                q_transposes(0)
                q_unit(1, 1, range(1))
                scores_own(0)
                q_unit(1, 1, range(1, 4))
                pe.wait_ge(vz_ready, 4)
                scores_two(0)
                q_transposes(1)
                scores_own(1)
                scores_two(1)
                transposed_p(0)
                values(0)
                transposed_p(1)
                values(1)
                transposed_p(2)
                pe.wait_ge(o_lo, 2)
                pe.wait_ge(s_read, len(SOFTMAXES))
                wo_unit(0, range(2))
                transposed_p(3)
                values(2)
                transposed_p(4)
                wo_unit(0, range(2, 3))
                values(3)
                values(4)
                wo_unit(0, range(3, 4))
                pe.wait_ge(o_lo, 4)
                wo_unit(1)
                wo_unit(2)
                wo_unit(3)

            pe.wait_ge(ones_ready, 1)
            for _ in range(WARM_UP):
                matmul(ps[:, 0, 0:P], ones[:], ones[:], True, True)
            ffn(0)
            retention()
            ffn(1)
            ffn(2)
            attention()
            ffn(3)


def constants():
    f = np.float32
    freq = (f(1.0) / (f(10000.0) ** np.linspace(0.0, 1.0, DK // 2, dtype=f))).astype(f)
    ang = (np.arange(T, dtype=f)[None, :] * freq[:, None]).astype(f)
    rot = np.stack([np.cos(ang), np.sin(ang)], axis=1).astype(f)
    lg = np.log(1.0 - 2.0 ** (-5.0 - np.arange(HEADS_R, dtype=np.float64)))
    diff = np.arange(T)[None, None, :] - np.arange(P)[:, None, None]
    decay = np.where(diff >= 0, np.exp(np.maximum(diff, 0) * lg[None, :, None]), 0.0).astype(f)
    inv = (f(1.0) / (f(10000.0) ** (np.arange(0, HD, 2, dtype=f) / f(HD)))).astype(f)
    ang = (np.arange(T, dtype=f)[:, None] * inv[None, :]).astype(f)
    cos, sin = np.cos(ang), np.sin(ang)
    rope = np.stack([np.concatenate([cos, cos], 1), np.concatenate([-sin, sin], 1)]).astype(f)
    rope = rope.reshape(2, 2, P, HD).transpose(2, 0, 1, 3)
    rel = np.arange(P)[:, None] + P - np.arange(2 * P)[None, :]
    mask = np.where((rel >= 0) & (rel < P), 0.0, NEG).astype(f)
    return rot, decay, np.ascontiguousarray(rope), mask, np.eye(P, dtype=f)


def kernel(**inputs):
    import concourse.bacc as bacc
    from concourse.bass_utils import run_bass_kernel_spmd

    a = {k: np.asarray(v) for k, v in inputs.items()}
    x_t = a["x"][0].T.reshape(DT, P, T).transpose(1, 0, 2)
    norms = [a["ffn1_norm"][0], a["mix_norm"][0], a["ffn2_norm"][0], a["ffn1_norm"][1], a["mix_norm"][1],
             a["ffn2_norm"][1], a["kv_norm"]]
    gains = np.concatenate([g.reshape(DT, P).T for g in norms], axis=1)
    ins = [a["ffn1_w_in"][0], a["ffn2_w_in"][0], a["ffn1_w_in"][1], a["ffn2_w_in"][1]]
    w_in = np.concatenate([w.reshape(2, 4, P, 2, GROUPS, 2, P).transpose(4, 0, 2, 1, 3, 5, 6).reshape(-1, P, UNIT)
                           for w in ins])
    outs = [a["ffn1_w_out"][0], a["ffn2_w_out"][0], a["ffn1_w_out"][1], a["ffn2_w_out"][1]]
    w_out = np.concatenate([w.reshape(2, FT // 2, P, DT, P).transpose(3, 0, 2, 1, 4).reshape(-1, P, OUT_UNIT)
                            for w in outs])
    wr = a["ret_w_in"][0]
    qk = [wr[:, j * HEADS_R * DK:(j + 1) * HEADS_R * DK].reshape(DT, P, HEADS_R, P, 2).transpose(2, 1, 0, 4, 3)
          .reshape(HEADS_R, 1, P, UNIT) for j in range(2)]
    v, g = (wr[:, 2 * HEADS_R * DK + j * HEADS_R * DV:][:, :HEADS_R * DV] for j in range(2))
    v = v.reshape(2, 4, P, HEADS_R, DV).transpose(3, 0, 2, 1, 4).reshape(HEADS_R, 2, P, UNIT)
    g = g.reshape(DT, P, HEADS_R, 2, 2, P).transpose(2, 3, 1, 0, 4, 5).reshape(HEADS_R, 2, P, UNIT)
    w_ret = np.concatenate([qk[0], qk[1], v, g], axis=1).reshape(-1, P, UNIT)
    w_ret_out = a["ret_w_out"][0].reshape(YT, P, DT, P).transpose(2, 1, 0, 3).reshape(-1, P, UNIT)
    w_kv = a["kv_w"].reshape(DT, P, 2 * KVH * HD).transpose(1, 0, 2).reshape(1, P, UNIT)
    w_q = a["attn_w_q"][0].reshape(2, 4, P, 2, 512).transpose(3, 0, 2, 1, 4).reshape(-1, P, UNIT)
    w_o = a["attn_w_o"][0].reshape(2, 4, P, DT, P)
    w_o = np.concatenate([w_o[:, :, :, 0:4].transpose(0, 2, 3, 1, 4).reshape(2, P, UNIT),
                          w_o[:, :, :, 4:8].reshape(DT, P, 2, 2, P).transpose(2, 1, 3, 0, 4).reshape(2, P, UNIT)])
    rot, decay, rope, mask, ident = constants()
    swapped = [(n, np.concatenate([n[HD // 2:], n[:HD // 2]])) for n in (a["q_norm"][0], a["k_norm"])]
    head_gains = np.broadcast_to(np.stack([np.stack(s) for s in swapped])[None], (P, 2, 2, HD))
    sinks = np.broadcast_to(a["attn_sinks"][0][None], (P, HEADS_Q))

    arrays = dict(x_t=x_t, gains=gains, w_in=w_in, w_out=w_out, w_ret=w_ret, w_ret_out=w_ret_out, w_kv=w_kv,
                  w_q=w_q, w_o=w_o, rot=rot, decay=decay, rope=rope, head_gains=head_gains, mask=mask, sinks=sinks,
                  ident=ident)
    nc = bacc.Bacc("TRN2", target_bir_lowering=False, num_devices=1)
    feeds, args = {}, []
    for name, arr in arrays.items():
        arr = np.ascontiguousarray(arr)
        feeds[f"{name}_dram"] = arr
        args.append(nc.dram_tensor(f"{name}_dram", arr.shape, mybir.dt.from_np(arr.dtype), kind="ExternalInput").ap())
    out = nc.dram_tensor("out_dram", (P, DT, T), F32, kind="ExternalOutput").ap()
    trunk(nc, *args, out)
    r = run_bass_kernel_spmd(nc, [feeds], core_ids=[0])
    got = r.results[0]["out_dram"]
    return np.ascontiguousarray(got.transpose(2, 1, 0).reshape(1, T, D))
```
